# Optimizing a Trainium2 kernel written in Bass

```python
import math
import jax, jax.numpy as jnp
from jax import lax
import numpy as np

D_MODEL = 1024
BATCH = 1
SEQ = 1024
DEPTH = 1
DEC_BATCH = 8
DEC_SEQ = 4
PAST_LEN = 8192
PAGE_SIZE = 128

N_META = 16
GLA_HEADS = 4
GLA_DK = D_MODEL // 16
GLA_DV = D_MODEL // 8
GLA_RANK = 16
GLA_TAU = 16.0
GLA_CHUNK = 64
DIFF_HEADS = 4
DIFF_DQK = D_MODEL // 16
DIFF_DV = 2 * DIFF_DQK
Q_BLOCK = 128
GLA_QK_W = GLA_HEADS * GLA_DK
GLA_WIDTH = GLA_HEADS * GLA_DV
DIFF_QK_W = DIFF_HEADS * 2 * DIFF_DQK
DIFF_WIDTH = DIFF_HEADS * DIFF_DV
MIX_WIDTH = GLA_WIDTH + DIFF_WIDTH
IN_SPLITS = (GLA_QK_W, GLA_QK_W, GLA_WIDTH, GLA_WIDTH, GLA_RANK, DIFF_QK_W, DIFF_QK_W, DIFF_WIDTH)
IN_WIDTH = sum(IN_SPLITS)
N_GROUPS = 4
EXPERTS_PER_GROUP = 8
N_EXPERTS = N_GROUPS * EXPERTS_PER_GROUP
TOP_K = 2
D_EXPERT = D_MODEL // 2
MOE_BLOCK = 128
EPS = 1e-6

kernel_name = "hymba_gla_diffattn_hmoe_step"

def rms_norm(x, gain):
    xf = x.astype(jnp.float32)
    y = xf * lax.rsqrt(jnp.mean(xf * xf, axis=-1, keepdims=True) + EPS)
    return (y * gain.astype(jnp.float32)).astype(x.dtype)

def split_cols(z):
    offs, acc = [], 0
    for w in IN_SPLITS[:-1]:
        acc += w
        offs.append(acc)
    return jnp.split(z, offs, axis=-1)

def mixer_inputs(xn, w_in, w_gk2, b_gk2, q_gain, k_gain):
    B, T, _ = xn.shape
    gq, gk, gv, gg, glr, dq, dk, dv = split_cols(xn @ w_in)
    gq = gq.reshape(B, T, GLA_HEADS, GLA_DK) * (GLA_DK ** -0.5)
    gk = gk.reshape(B, T, GLA_HEADS, GLA_DK)
    gv = gv.reshape(B, T, GLA_HEADS, GLA_DV)
    glog = jax.nn.log_sigmoid((glr @ w_gk2 + b_gk2).astype(jnp.float32)) / GLA_TAU
    glog = glog.reshape(B, T, GLA_HEADS, GLA_DK)
    dq = rms_norm(dq.reshape(B, T, DIFF_HEADS, 2, DIFF_DQK), q_gain)
    dk = rms_norm(dk.reshape(B, T, DIFF_HEADS, 2, DIFF_DQK), k_gain).reshape(B, T, DIFF_HEADS, 2 * DIFF_DQK)
    dv = dv.reshape(B, T, DIFF_HEADS, DIFF_DV)
    return (gq, gk, gv, glog, gg), (dq, dk, dv)

def gla_chunked(q, k, v, glog, s0, chunk):
    B, T, H, _ = q.shape
    nc = T // chunk

    def to_chunks(a):
        return jnp.moveaxis(a.astype(jnp.float32).reshape(B, nc, chunk, H, a.shape[-1]), 1, 0)

    causal = jnp.tril(jnp.ones((chunk, chunk), bool))[None, :, :, None, None]

    def step(s, inp):
        qc, kc, vc, gc = inp
        b = jnp.cumsum(gc, axis=1)
        o_inter = jnp.einsum('bchk,bhkv->bchv', qc * jnp.exp(b), s)
        rel = b[:, :, None] - b[:, None, :]
        decay = jnp.exp(jnp.where(causal, rel, -jnp.inf))
        a = jnp.einsum('bihk,bjhk,bijhk->bhij', qc, kc, decay)
        o_intra = jnp.einsum('bhij,bjhv->bihv', a, vc)
        b_last = b[:, -1]
        k_dec = kc * jnp.exp(b_last[:, None] - b)
        s_new = jnp.exp(b_last)[..., None] * s + jnp.einsum('bchk,bchv->bhkv', k_dec, vc)
        return s_new, o_inter + o_intra

    s_fin, o = lax.scan(step, s0.astype(jnp.float32), (to_chunks(q), to_chunks(k), to_chunks(v), to_chunks(glog)))
    return jnp.moveaxis(o, 0, 1).reshape(B, T, H, v.shape[-1]), s_fin

def diff_scores(q, k):
    B, Tk, H, _ = k.shape
    kk = k.reshape(B, Tk, H, 2, DIFF_DQK)
    return jnp.einsum('bqhcd,bkhcd->bhcqk', q, kk).astype(jnp.float32) * (DIFF_DQK ** -0.5)

def diff_probs(s, mask, lam):
    p = jax.nn.softmax(jnp.where(mask, s, -jnp.inf), axis=-1)
    return p[:, :, 0] - lam * p[:, :, 1]

def diff_attn_prompt(q, k, v, lam):
    B, T = q.shape[:2]
    n_blk = -(-T // Q_BLOCK)
    tp = n_blk * Q_BLOCK
    qp = jnp.pad(q, ((0, 0), (0, tp - T), (0, 0), (0, 0), (0, 0)))
    qb = jnp.moveaxis(qp.reshape(B, n_blk, Q_BLOCK, DIFF_HEADS, 2, DIFF_DQK), 1, 0)
    kpos = jnp.arange(T)

    def block(args):
        qblk, i = args
        qpos = i * Q_BLOCK + jnp.arange(Q_BLOCK)
        w = diff_probs(diff_scores(qblk, k), qpos[:, None] >= kpos[None, :], lam)
        return jnp.einsum('bhqk,bkhv->bqhv', w, v.astype(jnp.float32))

    o = lax.map(block, (qb, jnp.arange(n_blk)))
    return jnp.moveaxis(o, 0, 1).reshape(B, tp, DIFF_HEADS, DIFF_DV)[:, :T]

def diff_attn_sample(q, k_new, v_new, k_past, v_past, lam):
    tn, p = q.shape[1], k_past.shape[1]
    s = jnp.concatenate([diff_scores(q, k_past), diff_scores(q, k_new)], axis=-1)
    mask = jnp.concatenate([jnp.ones((tn, p), bool), jnp.tril(jnp.ones((tn, tn), bool))], axis=1)
    w = diff_probs(s, mask, lam)
    return (jnp.einsum('bhqk,bkhv->bqhv', w[..., :p], v_past.astype(jnp.float32))
            + jnp.einsum('bhqk,bkhv->bqhv', w[..., p:], v_new.astype(jnp.float32)))

def merge_heads(o_gla, gg, o_diff, gla_gain, diff_gain, lam_init, w_out, dt):
    B, T = o_gla.shape[:2]
    a = rms_norm(o_gla, gla_gain) * jax.nn.silu(gg.reshape(B, T, GLA_HEADS, GLA_DV).astype(jnp.float32))
    d = rms_norm(o_diff, diff_gain) * (1.0 - lam_init)
    cat = jnp.concatenate([a.reshape(B, T, GLA_WIDTH), d.reshape(B, T, DIFF_WIDTH)], axis=-1).astype(dt)
    return cat @ w_out

def grouped_experts(xf, eidx, gates, w1, w3, w2):
    n, d = xf.shape
    m = n * TOP_K
    e = eidx.reshape(m)
    tok = jnp.repeat(jnp.arange(n, dtype=jnp.int32), TOP_K)
    gate = gates.reshape(m)
    order = jnp.argsort(e)
    e_s, tok_s, gate_s = e[order], tok[order], gate[order]
    counts = jnp.bincount(e, length=N_EXPERTS)
    padded = (counts + MOE_BLOCK - 1) // MOE_BLOCK * MOE_BLOCK
    pad_end = jnp.cumsum(padded)
    pad_start = pad_end - padded
    start = jnp.cumsum(counts) - counts
    dest = pad_start[e_s] + jnp.arange(m) - start[e_s]
    n_blk = -(-(m + N_EXPERTS * (MOE_BLOCK - 1)) // MOE_BLOCK)
    cap = n_blk * MOE_BLOCK
    slot_tok = jnp.full((cap,), n, jnp.int32).at[dest].set(tok_s)
    blk_expert = jnp.minimum(jnp.searchsorted(pad_end, jnp.arange(n_blk) * MOE_BLOCK, side='right'), N_EXPERTS - 1)
    x_pad = jnp.concatenate([xf, jnp.zeros((1, d), xf.dtype)], axis=0)
    xb = x_pad[slot_tok].reshape(n_blk, MOE_BLOCK, d)

    def run(args):
        xblk, ei = args
        h = jax.nn.silu(xblk @ w1[ei]) * (xblk @ w3[ei])
        return h @ w2[ei]

    yb = lax.map(run, (xb, blk_expert)).reshape(cap, d)
    contrib = yb[dest] * gate_s[:, None].astype(yb.dtype)
    return jnp.zeros((n, d), yb.dtype).at[tok_s].add(contrib)

def hier_moe(x, w_rg, b_rg, w_re, b_re, w1, w3, w2):
    B, T, D = x.shape
    n = B * T
    xf = x.reshape(n, D)
    lg = (xf @ w_rg + b_rg).astype(jnp.float32)
    g = jnp.argmax(lg, axis=-1)
    g_gate = jnp.take_along_axis(jax.nn.softmax(lg, axis=-1), g[:, None], axis=-1)
    le = (xf @ w_re + b_re).astype(jnp.float32).reshape(n, N_GROUPS, EXPERTS_PER_GROUP)
    le_g = jnp.take_along_axis(le, g[:, None, None], axis=1)[:, 0]
    top_v, top_i = lax.top_k(le_g, TOP_K)
    gates = g_gate * jax.nn.softmax(top_v, axis=-1)
    eidx = g[:, None].astype(jnp.int32) * EXPERTS_PER_GROUP + top_i.astype(jnp.int32)
    return grouped_experts(xf, eidx, gates, w1, w3, w2).reshape(B, T, D).astype(x.dtype)

def setup_inputs(seed: int = 0) -> dict:
    key = jax.random.key(seed)
    ks = jax.random.split(key, 32)
    n_pages = PAST_LEN // PAGE_SIZE
    n_used = DEC_BATCH * n_pages
    n_phys = (5 * n_used + 3) // 4
    L = DEPTH

    def nrm(k, shape, scale):
        return jax.random.normal(k, shape, jnp.float32) * scale

    page_table = jax.random.permutation(ks[0], n_phys)[:n_used].reshape(DEC_BATCH, n_pages).astype(jnp.int32)
    return {
        "x_prompt": nrm(ks[1], (BATCH, SEQ, D_MODEL), 1.0),
        "x_sample": nrm(ks[2], (DEC_BATCH, DEC_SEQ, D_MODEL), 1.0),
        "cache_k": nrm(ks[3], (n_phys, PAGE_SIZE, L, DIFF_HEADS, 2 * DIFF_DQK), 1.0),
        "cache_v": nrm(ks[4], (n_phys, PAGE_SIZE, L, DIFF_HEADS, DIFF_DV), 1.0),
        "state_gla": nrm(ks[5], (DEC_BATCH, L, GLA_HEADS, GLA_DK, GLA_DV), 0.3),
        "page_table": page_table,
        "meta_tokens": nrm(ks[6], (N_META, D_MODEL), 1.0),
        "norm1": 1.0 + nrm(ks[7], (L, D_MODEL), 0.02),
        "w_in": nrm(ks[8], (L, D_MODEL, IN_WIDTH), D_MODEL ** -0.5),
        "w_gk2": nrm(ks[9], (L, GLA_RANK, GLA_QK_W), GLA_RANK ** -0.5),
        "b_gk2": nrm(ks[10], (L, GLA_QK_W), 0.1),
        "gla_norm": 1.0 + nrm(ks[11], (L, GLA_DV), 0.02),
        "q_norm": 1.0 + nrm(ks[12], (L, 2, DIFF_DQK), 0.02),
        "k_norm": 1.0 + nrm(ks[13], (L, 2, DIFF_DQK), 0.02),
        "lam_q1": nrm(ks[14], (L, DIFF_DQK), 0.1),
        "lam_k1": nrm(ks[15], (L, DIFF_DQK), 0.1),
        "lam_q2": nrm(ks[16], (L, DIFF_DQK), 0.1),
        "lam_k2": nrm(ks[17], (L, DIFF_DQK), 0.1),
        "diff_norm": 1.0 + nrm(ks[18], (L, DIFF_DV), 0.02),
        "w_out": nrm(ks[19], (L, MIX_WIDTH, D_MODEL), MIX_WIDTH ** -0.5),
        "norm2": 1.0 + nrm(ks[20], (L, D_MODEL), 0.02),
        "w_route_group": nrm(ks[21], (L, D_MODEL, N_GROUPS), D_MODEL ** -0.5),
        "b_route_group": nrm(ks[22], (L, N_GROUPS), 0.01),
        "w_route_expert": nrm(ks[23], (L, D_MODEL, N_EXPERTS), D_MODEL ** -0.5),
        "b_route_expert": nrm(ks[24], (L, N_EXPERTS), 0.01),
        "w_up": nrm(ks[25], (L, N_EXPERTS, D_MODEL, D_EXPERT), D_MODEL ** -0.5),
        "w_gate": nrm(ks[26], (L, N_EXPERTS, D_MODEL, D_EXPERT), D_MODEL ** -0.5),
        "w_down": nrm(ks[27], (L, N_EXPERTS, D_EXPERT, D_MODEL), D_EXPERT ** -0.5),
    }

def reference(x_prompt, x_sample, cache_k, cache_v, state_gla, page_table,
              meta_tokens, norm1, w_in, w_gk2, b_gk2, gla_norm, q_norm, k_norm,
              lam_q1, lam_k1, lam_q2, lam_k2, diff_norm, w_out, norm2,
              w_route_group, b_route_group, w_route_expert, b_route_expert,
              w_up, w_gate, w_down):
    B = x_prompt.shape[0]
    DB = x_sample.shape[0]
    dt = x_prompt.dtype
    hp = jnp.concatenate([jnp.broadcast_to(meta_tokens.astype(dt)[None], (B, N_META, D_MODEL)), x_prompt], axis=1)
    hs = x_sample
    pad = GLA_CHUNK - N_META
    past = page_table.shape[1] * PAGE_SIZE
    kp_l, vp_l, sp_l, ks_l, vs_l, ss_l = [], [], [], [], [], []
    for l in range(DEPTH):
        lam_init = 0.8 - 0.6 * math.exp(-0.3 * l)
        lam = (jnp.exp(jnp.sum(lam_q1[l].astype(jnp.float32) * lam_k1[l].astype(jnp.float32)))
               - jnp.exp(jnp.sum(lam_q2[l].astype(jnp.float32) * lam_k2[l].astype(jnp.float32))) + lam_init)

        xn = rms_norm(hp, norm1[l])
        (gq, gk, gv, glog, gg), (dq, dk, dv) = mixer_inputs(xn, w_in[l], w_gk2[l], b_gk2[l], q_norm[l], k_norm[l])

        def padf(a):
            return jnp.pad(a, ((0, 0), (pad, 0), (0, 0), (0, 0)))

        s0 = jnp.zeros((B, GLA_HEADS, GLA_DK, GLA_DV), jnp.float32)
        o_gla, s_fin = gla_chunked(padf(gq), padf(gk), padf(gv), padf(glog), s0, GLA_CHUNK)
        o_gla = o_gla[:, pad:]
        o_diff = diff_attn_prompt(dq, dk, dv, lam)
        hp = hp + merge_heads(o_gla, gg, o_diff, gla_norm[l], diff_norm[l], lam_init, w_out[l], dt)
        kp_l.append(dk)
        vp_l.append(dv)
        sp_l.append(s_fin)

        xn_s = rms_norm(hs, norm1[l])
        (gq, gk, gv, glog, gg), (dq, dk, dv) = mixer_inputs(xn_s, w_in[l], w_gk2[l], b_gk2[l], q_norm[l], k_norm[l])
        o_gla_s, s_new = gla_chunked(gq, gk, gv, glog, state_gla[:, l], hs.shape[1])
        k_past = cache_k[page_table, :, l].reshape(DB, past, DIFF_HEADS, 2 * DIFF_DQK)
        v_past = cache_v[page_table, :, l].reshape(DB, past, DIFF_HEADS, DIFF_DV)
        o_diff_s = diff_attn_sample(dq, dk, dv, k_past, v_past, lam)
        hs = hs + merge_heads(o_gla_s, gg, o_diff_s, gla_norm[l], diff_norm[l], lam_init, w_out[l], dt)
        ks_l.append(dk)
        vs_l.append(dv)
        ss_l.append(s_new)

        if l == DEPTH - 1:
            hp = hp[:, N_META:]
        hp = hp + hier_moe(rms_norm(hp, norm2[l]), w_route_group[l], b_route_group[l], w_route_expert[l],
                           b_route_expert[l], w_up[l], w_gate[l], w_down[l])
        hs = hs + hier_moe(rms_norm(hs, norm2[l]), w_route_group[l], b_route_group[l], w_route_expert[l],
                           b_route_expert[l], w_up[l], w_gate[l], w_down[l])

    y_prompt = hp
    y_sample = hs
    k_prompt = jnp.stack(kp_l, axis=2)
    v_prompt = jnp.stack(vp_l, axis=2)
    gla_prompt = jnp.stack(sp_l, axis=1)
    k_sample = jnp.stack(ks_l, axis=2)
    v_sample = jnp.stack(vs_l, axis=2)
    gla_sample = jnp.stack(ss_l, axis=1)
    return (y_prompt, y_sample, k_prompt, v_prompt, gla_prompt, k_sample, v_sample, gla_sample)


_drawn_inputs = setup_inputs


def setup_inputs(seed=0):
    import zlib

    import numpy as np

    out = dict(_drawn_inputs(seed))
    spreads = {}
    factors = {'gla_norm': 3.124,
     'k_norm': 7.551,
     'lam_q1': 9.705,
     'q_norm': 3.624,
     'diff_norm': 4.316,
     'norm2': 2.885,
     'b_route_group': 5.545,
     'b_route_expert': 5.44}
    for name, (base, spread) in spreads.items():
        noise = np.random.default_rng([zlib.crc32(name.encode()), seed]).standard_normal(out[name].shape)
        drawn = base * np.exp(spread * noise) if base else spread * noise
        out[name] = __import__('jax').numpy.asarray(drawn.astype(out[name].dtype))
    for name, factor in factors.items():
        out[name] = (out[name] * factor).astype(out[name].dtype)
    return out
```

```python
from contextlib import ExitStack

import numpy as np

import concourse.bass as bass
from concourse import mybir

F32 = mybir.dt.float32
F32R = mybir.dt.float32r
I32 = mybir.dt.int32
U32 = mybir.dt.uint32
ALU = mybir.AluOpType
ACT = mybir.ActivationFunctionType
X = mybir.AxisListType.X

P = 128
D = 1024
KD = D // P
SEQ, META, SAMPLES, STEPS = 1024, 16, 8, 4
NS = SAMPLES * STEPS
T0 = NS + META
TILES = 1 + SEQ // P
COLS = T0 + SEQ
HEADS, DK, DV, RANK = 4, 64, 128, 16
GW = HEADS * DK
W = HEADS * DV
EPS = 1e-6
NEG = -1e30
CLAMP = 43.0
LAM_INIT = 0.2
PAGE, PAGES, PHYS = 128, 64, 640
GROUP = 4
GROUPS = PAGES // GROUP
EXPERTS, NGROUPS, PER_GROUP, DE = 32, 4, 8, 512
NR = NGROUPS + EXPERTS
TOKENS = NS + SEQ
BLOCK = 128
SPARE = 16



def constant_table():
    t = np.arange(P)
    s, u = t[:, None], t[None, :]
    table = {}

    def put(name, a):
        a = np.asarray(a, np.float32)
        full = np.zeros((P, a.shape[1]), np.float32)
        full[:a.shape[0]] = a
        table[name] = full

    put("ident", np.eye(P))
    put("ones", np.ones((P, P)))
    upto = (s <= u)
    anchor0 = 32 * (u // 32) + 15
    anchor1 = 64 * (u // 64) + 31
    anchor2 = 0 * u + 63
    sixteenth = 1.0 / 16.0
    for n, anchor in enumerate((anchor0, anchor1, anchor2)):
        put(f"rel{n}", sixteenth * (upto.astype(int) - (s <= anchor)))
    put("cum", sixteenth * upto)
    put("rest", sixteenth * (s > u))
    put("tau", np.full((P, 1), sixteenth))
    put("pair0", (s // 32 == u // 32) & (s <= u))
    put("pair1", (s // 64 == u // 64) & (s % 64 < 32) & (u % 64 >= 32))
    put("pair2", (s < 64) & (u >= 64))
    put("causal", np.where(u <= s, 0.0, NEG))
    put("before", s < u)
    s, u = s[:NS], u[:, :NS]
    same = s // STEPS == u // STEPS
    put("s_rel", sixteenth * (same & (s <= u)) - sixteenth * (same & (s % STEPS <= 1)))
    put("s_cum", sixteenth * (same & (s <= u)))
    put("s_rest", sixteenth * (same & (s > u)))
    put("s_pair", same & (s <= u))
    put("s_of", s // STEPS == np.arange(SAMPLES)[None])
    put("s_tau", sixteenth * (s // STEPS == np.arange(SAMPLES)[None]))
    new = np.full((P, SAMPLES, NS), NEG, np.float32)
    for r in range(P):
        for b in range(SAMPLES):
            new[r, b, b * STEPS:b * STEPS + r % STEPS + 1] = 0.0
    put("new_mask", new.reshape(P, -1))
    row = np.ones((P, 1))
    put("first4", row * np.arange(NGROUPS, 0, -1)[None])
    put("first32", row * np.arange(EXPERTS, 0, -1)[None])
    put("iota32", row * np.arange(EXPERTS)[None])
    put("iota16", row * np.arange(SPARE)[None])
    valid = np.ones((P, TILES))
    valid[NS:, 0] = 0
    put("valid", valid)
    ids = NS + P * (np.arange(TILES)[None] - 1) + t[:, None]
    ids[:, 0] = t
    put("token", ids)
    put("in_page", (t % 32)[:, None])
    at, n = {}, 0
    for name, a in table.items():
        at[name] = (n, a.shape[1])
        n += a.shape[1]
    return at, np.concatenate(list(table.values()), 1)


CONST_AT, CONSTS = constant_table()


class Chain:

    def __init__(self, eng, sem):
        self.eng, self.sem, self.base, self.n = eng, sem, 0, 0

    def link(self, ins):
        self.n += 1
        ins.then_inc(self.sem, 1)
        self.eng.wait_ge(self.sem, self.base + self.n)
        return ins

    def loop(self, i, each):
        self.start, self.each = self.base + self.n, each
        self.base, self.n = self.start + i * each, 0

    def end(self, count):
        assert self.n == self.each, (self.n, self.each)
        self.base, self.n = self.start + count * self.each, 0


class Space:
    pass


def const(k, name, rows=P):
    a, n = CONST_AT[name]
    return k.ident[0:rows, 0:n] if name == "ident" else k.consts[0:rows, a - P:a - P + n]


def cols(i):
    return slice(0, T0) if i == 0 else slice(T0 + P * (i - 1), T0 + P * i)




def project(nc, k, io):
    CHUNKS = [("glr", 1536, RANK), ("qk", 0, W), ("v", GW * 2, W), ("gate", 1024, W),
              ("dq", 1552, W), ("dk", 2064, W), ("dv", 2576, W)]
    WIDE = CHUNKS[1:]
    BY = {"qk": "act", "v": "dve", "gate": "act", "dq": "dve", "dk": "dve", "dv": "act"}
    ACC = 6
    w_in = io["w_in"][0].rearrange("(p k) n -> p k n", k=KD)
    x_rows = io["x_prompt"][0].rearrange("(i p) d -> i p d", p=P)
    k_rows = io["k_prompt"].rearrange("a n l h d -> (a n) (l h d)")
    v_rows = io["v_prompt"].rearrange("a n l h d -> (a n) (l h d)")
    ks_rows = io["k_sample"].rearrange("a n l h d -> (a n) (l h d)")
    vs_rows = io["v_sample"].rearrange("a n l h d -> (a n) (l h d)")

    GLR = [(0, 512), (512, 512), (1024, COLS - 1024)]
    STORED = [(1, i) for i in range(1, TILES)] + [(2, i) for i in range(TILES)] + [(5, i) for i in range(1, TILES)]

    def unit(c, i):
        return c * TILES + i

    def freed(u):
        by = BY[WIDE[u // TILES][0]]
        return by, sum(BY[WIDE[x // TILES][0]] == by for x in range(u + 1))

    with ExitStack() as ctx:
        def sb(name, shape, dt=F32):
            return ctx.enter_context(nc.sbuf_tensor(name, shape, dt))

        sem = k.sem
        xh, xl = sb("xh", [P, KD, COLS], F32R), sb("xl", [P, KD, COLS], F32R)
        w = sb("w", [P, KD, W])
        wh, wl = sb("wh", [P, KD, W], F32R), sb("wl", [P, KD, W], F32R)
        wlrs = sb("wlrs", [P, KD, 2 * RANK], F32R)
        st = sb("st", [P, 2, W])
        gain_qk = sb("gain_qk", [P, 2, P])
        ss = sb("ss", [P, 2 * TILES])
        sq = sb("sq", [P, W])
        kn = sb("kn", [P, 2, W])
        s8 = sb("s8", [P, 2, 8])
        x_in = k.kT[:].rearrange("p h t -> p (h t)").rearrange("p (s n) -> p s n", n=D)
        log_scratch = k.kT[:].rearrange("p h t -> p (h t)")
        scratch = k.qT[:].rearrange("p h t -> p (h t)")
        squares, gain1 = scratch[:, 0:D], scratch[:, D:2 * D]
        lrT = scratch[0:2 * RANK, 2 * D:2 * D + COLS]
        at = 2 * D + COLS
        bgk, wgk = scratch[:, at:at + GW], scratch[0:2 * RANK, at + GW:at + 2 * GW]
        wlr = scratch[:, at + 2 * GW:at + 2 * GW + KD * RANK].rearrange("p (k n) -> p k n", k=KD)

        s_const, s_gain, s_lr, s_gk = sem("p_const"), sem("p_gain"), sem("p_lr"), sem("p_gk")
        s_x = [sem(f"p_x{j}") for j in range(4)]
        s_w, s_hi, s_lo, s_used = sem("p_w"), sem("p_hi"), sem("p_lo"), sem("p_used")
        s_xh, s_lrs, s_st = sem("p_xh"), sem("p_lrs"), [sem("p_st0"), sem("p_st1")]
        s_sum, s_ms, s_root, s_xn = sem("p_sum"), sem("p_ms"), sem("p_root"), sem("p_xn")
        s_turn, s_xT = sem("p_turn"), sem("p_xT")
        s_acc, s_dve, s_act = sem("p_acc"), sem("p_free_dve"), sem("p_free_act")
        s_lrp, s_lrT, s_z, s_zs = sem("p_lrp"), sem("p_lrT"), sem("p_z"), sem("p_zs")
        s_sq, s_s8, s_r8, s_kn, s_qkt, s_qkT = (sem("p_sq"), sem("p_s8"), sem("p_r8"), sem("p_kn"),
                                                sem("p_qkt"), sem("p_qkT"))
        s_ln, s_ch, s_out, s_ko = sem("p_ln"), sem("p_ch"), sem("p_out"), [sem("p_ko0"), sem("p_ko1")]
        s_rest = sem("p_rest")
        s_gqk, s_ach = sem("p_gqk"), sem("p_ach")
        QK = [(c, i) for c in (3, 4) for i in range(TILES)]

        with nc.Block() as block:
            @block.sync
            def _(sp):
                sp.dma_start(k.ident[:], io["consts"][:, 0:P]).then_inc(s_const, 16)
                sp.dma_start(gain1, io["norm1"].to_broadcast([P, D])).then_inc(s_gain, 16)

                def load_x(i):
                    if i >= 4:
                        sp.wait_ge(s_turn, 2 * (i - 3))
                    if i == 0:
                        sp.dma_start(x_in[0:NS, 0, :], io["x_sample"].rearrange("b t d -> (b t) d")).then_inc(s_x[0], 16)
                        sp.dma_start(x_in[NS:T0, 0, :], io["meta_tokens"]).then_inc(s_x[0], 16)
                    else:
                        sp.dma_start(x_in[:, i % 4, :], x_rows[i - 1]).then_inc(s_x[i % 4], 16)

                def load_w(c):
                    if c:
                        sp.wait_ge(s_lo, KD * c)
                    _, a, n = WIDE[c]
                    sp.dma_start(w[:], w_in[:, :, a:a + n]).then_inc(s_w, 16)

                def wait_kept(c, i):
                    by, n = freed(unit(c, i))
                    sp.wait_ge(s_dve if by == "dve" else s_act, n)

                load_x(0)
                load_w(0)
                for i in range(1, 4):
                    load_x(i)
                sp.dma_start(k.consts[:], io["consts"][:, P:]).then_inc(s_rest, 16)
                sp.dma_start(wlr, w_in[:, :, CHUNKS[0][1]:CHUNKS[0][1] + RANK]).then_inc(s_lr, 16)
                for half in range(2):
                    sp.dma_start(wgk[RANK * half:RANK * (half + 1)], io["w_gk2"][0]).then_inc(s_gk, 16)
                sp.dma_start(bgk, io["b_gk2"].to_broadcast([P, GW])).then_inc(s_gk, 16)
                for n, g in enumerate(("q_norm", "k_norm")):
                    sp.dma_start(gain_qk[:, n, :], io[g].rearrange("a c d -> a (c d)").to_broadcast([P, P])).then_inc(s_gqk, 16)
                for i in range(4, TILES):
                    load_x(i)
                load_w(1)
                for c in range(1, len(WIDE)):
                    if c + 1 < len(WIDE):
                        load_w(c + 1)
                    for i in range(TILES):
                        if (c, i) in STORED:
                            m = STORED.index((c, i))
                            to = {1: k.v_d, 2: k.gate_d}.get(c)
                            r = NS if i == 0 else P
                            to = v_rows[META + P * (i - 1):META + P * i] if to is None else to[i, 0:r]
                            wait_kept(c, i)
                            sp.dma_start(to, st[0:r, m % 2, :]).then_inc(s_st[m % 2], 16)
                        elif c == 5:
                            wait_kept(c, i)
                            sp.dma_start(vs_rows, k.new_v[:]).then_inc(s_out, 16)
                            sp.dma_start(v_rows[0:META], k.meta_dv[:]).then_inc(s_out, 16)
                        elif c == 4:
                            n = len(QK) // 2 + i
                            sp.wait_ge(s_kn, n + 1)
                            if i == 0:
                                sp.dma_start(ks_rows, kn[0:NS, n % 2, :]).then_inc(s_ko[n % 2], 16)
                                sp.dma_start(k_rows[0:META], kn[NS:T0, n % 2, :]).then_inc(s_ko[n % 2], 16)
                            else:
                                sp.dma_start(k_rows[META + P * (i - 1):META + P * i], kn[:, n % 2, :]).then_inc(s_ko[n % 2], 16)
                sp.wait_ge(s_rest, 16)
                sp.wait_ge(s_out, 32)
                sp.wait_ge(s_st[0], 16 * ((len(STORED) + 1) // 2))
                sp.wait_ge(s_st[1], 16 * (len(STORED) // 2))
                sp.wait_ge(s_ko[0], 16 * 4)
                sp.wait_ge(s_ko[1], 16 * 6)

            @block.tensor
            def _(pe):
                pe.wait_ge(s_const, 16)
                ident = const(k, "ident")

                def turn_x(i):
                    rows = T0 if i == 0 else P
                    pe.wait_ge(s_xn, i + 1)
                    xk = x_in[0:rows, i % 4, :].rearrange("p (d k) -> p k d", k=KD)
                    for half in range(2):
                        if i:
                            pe.wait_ge(s_xT, 2 * i + half - 1)
                        for j in range(4):
                            mm = pe.transpose(k.ps[:, 6 + half, j * P:j * P + rows], xk[:, 4 * half + j, :], ident[0:rows, 0:rows])
                        mm.then_inc(s_turn, 1)

                def products(out, cols_, w_high, w_low, kk, first, last):
                    pe.matmul(out, xh[:, kk, cols_], w_high[:, kk, :], start=first, stop=False)
                    pe.matmul(out, xh[:, kk, cols_], w_low[:, kk, :], start=False, stop=False)
                    return pe.matmul(out, xl[:, kk, cols_], w_high[:, kk, :], start=False, stop=last)

                def decays():
                    pe.wait_ge(s_xT, 2 * TILES)
                    pe.wait_ge(s_lrs, 2)
                    for n, (a, m) in enumerate(GLR):
                        if n == 2:
                            pe.wait_ge(s_lrT, 1)
                        for kk in range(KD):
                            for x in (xh, xl):
                                mm = pe.matmul(k.ps[0:2 * RANK, 6 + n % 2, 0:m], wlrs[:, kk, :], x[:, kk, a:a + m],
                                               start=kk == 0 and x is xh, stop=kk == KD - 1 and x is xl)
                        mm.then_inc(s_lrp, 1)
                    pe.wait_ge(s_lrT, 3)
                    pe.wait_ge(s_gk, 48)
                    for i in range(TILES):
                        rows = T0 if i == 0 else P
                        if i >= 2:
                            pe.wait_ge(s_zs, i - 1)
                        pe.matmul(k.ps[0:rows, 6 + i % 2, 0:GW], lrT[:, cols(i)], wgk, start=True, stop=True).then_inc(s_z, 1)

                turned = 0

                def turn(n):
                    c, i = QK[n]
                    rows = T0 if i == 0 else P
                    pe.wait_ge(s_kn, n + 1)
                    if n >= 2:
                        pe.wait_ge(s_qkT, n - 1)
                    for h in range(HEADS):
                        mm = pe.transpose(k.ps[:, 6 + n % 2, h * P:h * P + rows], kn[0:rows, n % 2, h * P:(h + 1) * P], ident[0:rows, 0:rows])
                    mm.then_inc(s_qkt, 1)

                turn_x(0)
                for c in range(len(WIDE)):
                    for i in range(TILES):
                        if c == 0:
                            if i + 1 < TILES:
                                turn_x(i + 1)
                            else:
                                decays()
                            pe.wait_ge(s_xT, 2 * i + 2)
                        u = unit(c, i)
                        rows = T0 if i == 0 else P
                        if u >= ACC:
                            by, n = freed(u - ACC)
                            pe.wait_ge(s_dve if by == "dve" else s_act, n)
                        for kk in range(KD):
                            if i == 0:
                                pe.wait_ge(s_lo, KD * c + kk + 1)
                            mm = products(k.ps[0:rows, u % ACC, :], cols(i), wh, wl, kk, kk == 0, kk == KD - 1)
                            if i == TILES - 1 and kk < KD - 1:
                                mm.then_inc(s_used, 1)
                        mm.then_inc(s_acc, 1)
                        if (c, i) in QK[2:] or (c, i) in ((5, 0), (5, 1)):
                            turn(turned)
                            turned += 1

            @block.scalar
            def _(act):
                chain = Chain(act, s_ach)

                def sum_squares(i):
                    rows = T0 if i == 0 else P
                    act.wait_ge(s_x[i % 4], 16 * (i // 4 + 1) + (16 if i % 4 == 0 else 0))
                    act.activation(squares[0:rows], x_in[0:rows, i % 4, :], ACT.Square, accum_out=ss[0:rows, i:i + 1]).then_inc(s_sum, 1)
                    act.wait_ge(s_ms, i + 1)
                    act.activation(ss[0:rows, TILES + i:TILES + i + 1], ss[0:rows, i:i + 1], ACT.Sqrt).then_inc(s_root, 1)

                def high_x(i):
                    rows = T0 if i == 0 else P
                    for half in range(2):
                        act.wait_ge(s_turn, 2 * i + half + 1)
                        act.copy(xh[:, 4 * half:4 * half + 4, cols(i)],
                                 k.ps[:, 6 + half, :].rearrange("p (j t) -> p j t", j=4)[:, :, 0:rows]).then_inc(s_xh, 1)

                def high_w(c):
                    act.wait_ge(s_w, 16 * (c + 1))
                    for kk in range(KD):
                        if c and kk < KD - 1:
                            act.wait_ge(s_used, (KD - 1) * (c - 1) + kk + 1)
                        elif c:
                            act.wait_ge(s_acc, unit(c - 1, TILES - 1) + 1)
                        act.copy(wh[:, kk, :], w[:, kk, :]).then_inc(s_hi, 1)

                def keep_low_rank():
                    for n, (a, m) in enumerate(GLR):
                        act.wait_ge(s_lrp, n + 1)
                        act.copy(lrT[:, a:a + m], k.ps[0:2 * RANK, 6 + n % 2, 0:m]).then_inc(s_lrT, 1)

                def log_sigmoid():
                    act.wait_ge(s_zs, TILES)
                    for rows, a, b in ((T0, 0, 1), (P, 1, TILES)):
                        t = log_scratch[0:rows, a * GW:b * GW]
                        z = k.z[0:rows, a:b, :].rearrange("p a n -> p (a n)")
                        chain.link(act.activation(t, z, ACT.Abs))
                        chain.link(act.activation(t, t, ACT.Exp, scale=-1.0))
                        act.activation(t, t, ACT.Ln, bias=1.0).then_inc(s_ln, 1)

                def qkT(n):
                    c, i = QK[n]
                    act.wait_ge(s_qkt, n + 1)
                    bank = k.ps[:, 6 + n % 2, :].rearrange("p (h t) -> p h t", h=HEADS)
                    to = k.qT if c == 3 else k.kT
                    if i:
                        act.copy(to[:, :, P * (i - 1):P * i], bank).then_inc(s_qkT, 1)
                    elif c == 3:
                        act.copy(k.qTs[:], bank[:, :, 0:NS]).then_inc(s_qkT, 1)
                    else:
                        act.copy(k.meta_kT[:], bank[:, :, NS:T0])
                        act.copy(k.kTs[:], bank[:, :, 0:NS]).then_inc(s_qkT, 1)

                def keep(c, i):
                    name, u = WIDE[c][0], unit(c, i)
                    rows = T0 if i == 0 else P
                    bank = k.ps[0:rows, u % ACC, :]
                    act.wait_ge(s_acc, u + 1)
                    meta = {"qk": k.meta_qk, "dv": k.meta_dv}.get(name)
                    if i == 0 and meta is not None:
                        act.copy(meta[:], bank[NS:T0])
                    r = NS if i == 0 else P
                    if (c, i) in STORED:
                        m = STORED.index((c, i))
                        if m >= 2:
                            act.wait_ge(s_st[m % 2], 16 * (m // 2))
                        to = st[0:r, m % 2, :]
                    else:
                        to = k.new_v[:] if name == "dv" else k.qk[0:r, i, :]
                    act.copy(to, bank[0:r]).then_inc(s_act, 1)

                kept = 0
                sum_squares(0)
                high_x(0)
                high_w(0)
                for i in range(1, TILES):
                    sum_squares(i)
                    high_x(i)
                    if i == 4:
                        act.wait_ge(s_lr, 16)
                        act.copy(wlrs[:, :, 0:RANK], wlr).then_inc(s_lrs, 1)
                    if i >= 2:
                        keep(0, i - 2)
                for c, (name, _, _) in enumerate(WIDE):
                    for i in range(TILES):
                        u = unit(c, i)
                        rows = T0 if i == 0 else P
                        bank = k.ps[0:rows, u % ACC, :]
                        if (c, i) == (0, TILES - 1):
                            keep_low_rank()
                        if i == TILES - 1 and c + 1 < len(WIDE):
                            high_w(c + 1)
                        if (c, i) == (1, 0):
                            log_sigmoid()
                        if name in ("qk", "gate", "dv"):
                            if c or i >= TILES - 2:
                                keep(c, i)
                        elif name in ("dq", "dk"):
                            n = QK.index((c, i))
                            act.wait_ge(s_acc, u + 1)
                            if n >= 1:
                                act.wait_ge(s_s8, n)
                            act.activation(sq[0:rows], bank, ACT.Square).then_inc(s_sq, 1)
                            act.wait_ge(s_s8, n + 1)
                            act.activation(s8[0:rows, n % 2, :], s8[0:rows, n % 2, :], ACT.Sqrt).then_inc(s_r8, 1)
                        if (c, i) in QK[2:] or (c, i) in ((5, 0), (5, 1)):
                            qkT(kept)
                            kept += 1

            @block.vector
            def _(dve):
                chain = Chain(dve, s_ch)

                def low_w(c):
                    for kk in range(KD):
                        dve.wait_ge(s_hi, KD * c + kk + 1)
                        dve.tensor_tensor(wl[:, kk, :], w[:, kk, :], wh[:, kk, :].bitcast(F32), ALU.subtract).then_inc(s_lo, 1)

                dve.wait_ge(s_gain, 16)
                for i in range(TILES):
                    rows = T0 if i == 0 else P
                    col = ss[0:rows, i:i + 1]
                    dve.wait_ge(s_sum, i + 1)
                    dve.tensor_scalar(col, col, 1.0 / D, EPS, ALU.mult, ALU.add).then_inc(s_ms, 1)
                    dve.wait_ge(s_root, i + 1)
                    root = ss[0:rows, TILES + i:TILES + i + 1]
                    chain.link(dve.reciprocal(root, root))
                    x = x_in[0:rows, i % 4, :]
                    dve.scalar_tensor_tensor(out=x, in0=x, scalar=root, in1=gain1[0:rows], op0=ALU.mult, op1=ALU.mult).then_inc(s_xn, 1)
                    for half in range(2):
                        dve.wait_ge(s_xh, 2 * i + half + 1)
                        dve.tensor_tensor(xl[:, 4 * half:4 * half + 4, cols(i)],
                                          k.ps[:, 6 + half, :].rearrange("p (j t) -> p j t", j=4)[:, :, 0:rows],
                                          xh[:, 4 * half:4 * half + 4, cols(i)].bitcast(F32), ALU.subtract).then_inc(s_xT, 1)
                    if i == 0:
                        low_w(0)
                dve.wait_ge(s_lrs, 1)
                dve.tensor_tensor(wlrs[:, :, RANK:2 * RANK], wlr, wlrs[:, :, 0:RANK].bitcast(F32), ALU.subtract).then_inc(s_lrs, 1)
                dve.wait_ge(s_gk, 48)
                for i in range(TILES):
                    rows = T0 if i == 0 else P
                    dve.wait_ge(s_z, i + 1)
                    dve.tensor_tensor(k.z[0:rows, i, :], k.ps[0:rows, 6 + i % 2, 0:GW], bgk[0:rows], ALU.add).then_inc(s_zs, 1)
                low_w(1)
                dve.wait_ge(s_ln, 2)
                for rows, a, b in ((T0, 0, 1), (P, 1, TILES)):
                    t = log_scratch[0:rows, a * GW:b * GW]
                    z = k.z[0:rows, a:b, :].rearrange("p a n -> p (a n)")
                    chain.link(dve.scalar_tensor_tensor(out=z, in0=z, scalar=0.0, in1=t, op0=ALU.min, op1=ALU.subtract))
                chain.link(dve.tensor_copy(k.meta_z[:], k.z[NS:T0, 0, :]))
                for c, (name, _, _) in enumerate(WIDE):
                    for i in range(TILES):
                        u = unit(c, i)
                        rows = T0 if i == 0 else P
                        bank = k.ps[0:rows, u % ACC, :]
                        if c and i == TILES - 1 and c + 1 < len(WIDE):
                            low_w(c + 1)
                        if name == "v":
                            dve.wait_ge(s_acc, u + 1)
                            if i == 0:
                                dve.tensor_copy(k.meta_v[:], bank[NS:T0])
                                dve.tensor_copy(k.sample_v[:], bank[0:NS]).then_inc(s_dve, 1)
                            else:
                                m = STORED.index((c, i))
                                if m >= 2:
                                    dve.wait_ge(s_st[m % 2], 16 * (m // 2))
                                dve.tensor_copy(st[:, m % 2, :], bank).then_inc(s_dve, 1)
                        elif name in ("dq", "dk"):
                            n = QK.index((c, i))
                            eight = s8[0:rows, n % 2, :]
                            if n == 0:
                                dve.wait_ge(s_gqk, 32)
                            dve.wait_ge(s_sq, n + 1)
                            chain.link(dve.reduce_sum(eight, sq[0:rows].rearrange("p (g d) -> p g d", g=8), axis=X))
                            dve.tensor_scalar(eight, eight, 1.0 / DK, EPS, ALU.mult, ALU.add).then_inc(s_s8, 1)
                            dve.wait_ge(s_r8, n + 1)
                            chain.link(dve.reciprocal(eight, eight))
                            if n >= 2:
                                dve.wait_ge(s_qkt, n - 1)
                            if n - 2 >= TILES:
                                m = n - 2 - TILES
                                dve.wait_ge(s_ko[n % 2], 16 * (m // 2 + 1 + (1 if n % 2 == TILES % 2 else 0)))
                            out = kn[0:rows, n % 2, :].rearrange("p (g d) -> p g d", g=8)
                            dve.tensor_tensor(out, bank.rearrange("p (g d) -> p g d", g=8),
                                              eight.unsqueeze(2).to_broadcast([rows, 8, DK]), ALU.mult).then_inc(s_dve, 1)
                            dve.wait_ge(s_dve, freed(u)[1])
                            out = kn[0:rows, n % 2, :].rearrange("p (h x) -> p h x", h=HEADS)
                            dve.tensor_tensor(out, out, gain_qk[0:rows, c - 3, :].unsqueeze(1).to_broadcast([rows, HEADS, P]),
                                              ALU.mult).then_inc(s_kn, 1)




def linear_attention(nc, k, io):
    LV = 3
    with ExitStack() as ctx:
        def sb(name, shape, dt=F32):
            return ctx.enter_context(nc.sbuf_tensor(name, shape, dt))

        sem = k.sem
        lo = sb("g_lo", [P, 2, 2, LV, GW])
        end = sb("g_end", [P, 2, GW])
        q_st = sb("g_q_st", [P, 2, GW])
        k_st = sb("g_k_st", [P, 2, GW])
        turned = sb("g_turned", [DK, 2 * LV + 1, HEADS, P])
        pairs = sb("g_pairs", [P, LV, HEADS, P])
        states = [sb("g_state", [DK, HEADS, DV])[:], k.cat[0:DK, 1, W:D].rearrange("p (h n) -> p h n", h=HEADS)]
        last = sb("g_last", [DK, 2, HEADS])
        s_c, s_clip, s_e, s_d, s_q, s_t, s_tk = (sem("g_c"), sem("g_clip"), sem("g_e"), sem("g_d"), sem("g_q"),
                                                 sem("g_t"), sem("g_tk"))
        s_a, s_m, s_o, s_s, s_k, s_out, s_sch = (sem("g_a"), sem("g_m"), sem("g_o"), sem("g_s"), sem("g_k"),
                                                 sem("g_out"), sem("g_sch"))
        s_ok = sem("g_ok")
        flat = k.ps[:].rearrange("p b n -> p (b n)")
        s_v, s_dv = [sem("g_v0"), sem("g_v1")], sem("g_dv")
        s_zero, s_spare = sem("g_zero"), sem("g_spare")
        zeros = k.cat[:, TILES - 1, W:D]
        NB = 2 * LV + 1

        with nc.Block() as block:
            @block.tensor
            def _(pe):
                ident = const(k, "ident")

                def stage_a(i):
                    rows = META if i == 0 else P
                    z = k.meta_z[:] if i == 0 else k.z[:, i, :]
                    if i:
                        pe.wait_ge(s_q, i)
                        for n, name in ((0, "rel0"), (1, "rel1"), (2, "rel2"), (4, "cum")):
                            pe.matmul(flat[0:rows, n * GW:(n + 1) * GW], const(k, name), z, start=True, stop=True)
                    pe.matmul(flat[0:rows, 5 * GW:6 * GW], const(k, "rest", rows)[:, 0:rows], z, start=True, stop=True)
                    for h in range(HEADS):
                        mm = pe.matmul(flat[0:DK, 3 * GW + h:3 * GW + h + 1], z[:, h * DK:(h + 1) * DK], const(k, "tau", rows),
                                       start=True, stop=True)
                    mm.then_inc(s_c, 1)

                def turn(i, n):
                    if n >= 4:
                        pe.wait_ge(s_tk, (i - 1) * NB + n - 3)
                    src = lo[:, i % 2, 0, n, :] if n < LV else q_st[:, i % 2, :] if n == LV else lo[:, i % 2, 1, n - LV - 1, :]
                    for h in range(HEADS):
                        mm = pe.transpose(k.ps[0:DK, 3 + n % 4, h * P:(h + 1) * P], src[:, h * DK:(h + 1) * DK], ident)
                    mm.then_inc(s_t, 1)

                def stage_b(i):
                    rows = META if i == 0 else P
                    v = k.meta_v[:] if i == 0 else k.v[:, i, :]
                    pe.wait_ge(s_q, i + 1)
                    if i in (1, 5):
                        pe.wait_ge(s_v[i // 5], 16)
                    if i:
                        pe.wait_ge(s_s, i)
                    for h in range(HEADS):
                        mm = pe.matmul(k.ps[0:DK, 7, h * DV:(h + 1) * DV], k_st[0:rows, i % 2, h * DK:(h + 1) * DK],
                                       v[:, h * DV:(h + 1) * DV], start=True, stop=True)
                    mm.then_inc(s_k, 1)
                    if i == 0:
                        return
                    if i >= 2:
                        pe.wait_ge(s_ok, i - 1)
                    for n in range(NB):
                        turn(i, n)
                    for n in range(LV):
                        pe.wait_ge(s_tk, (i - 1) * NB + LV + 2 + n)
                        for h in range(HEADS):
                            mm = pe.matmul(k.ps[:, 3 + (n + 3) % 4, h * P:(h + 1) * P], turned[:, LV + 1 + n, h, :], turned[:, n, h, :],
                                           start=True, stop=True)
                        mm.then_inc(s_a, 1)
                    for h in range(HEADS):
                        out = k.ps[:, 5, h * DV:(h + 1) * DV]
                        pe.matmul(out, turned[:, LV, h, :], states[(i - 1) % 2][:, h, :], start=True, stop=False)
                        for n in range(LV):
                            if h == 0:
                                pe.wait_ge(s_m, (i - 1) * LV + n + 1)
                            mm = pe.matmul(out, pairs[:, n, h, :], v[:, h * DV:(h + 1) * DV], start=False, stop=n == LV - 1)
                    mm.then_inc(s_o, 1)

                stage_a(0)
                for i in range(TILES):
                    if i + 1 < TILES:
                        stage_a(i + 1)
                    stage_b(i)

            @block.scalar
            def _(act):
                def stage_a(i):
                    rows = META if i == 0 else P
                    act.wait_ge(s_c, i + 1)
                    if i:
                        act.wait_ge(s_q, i)
                    act.activation(end[0:rows, 1, :], flat[0:rows, 5 * GW:6 * GW], ACT.Exp)
                    if i:
                        act.activation(end[:, 0, :], flat[:, 4 * GW:5 * GW], ACT.Exp).then_inc(s_e, 1)
                        act.wait_ge(s_clip, 2 * i)
                    act.activation(last[:, i % 2, :], flat[0:DK, 3 * GW:3 * GW + HEADS], ACT.Exp).then_inc(s_d, 1)
                    if i:
                        act.activation(lo[:, i % 2, 0], lo[:, i % 2, 0], ACT.Exp).then_inc(s_e, 1)
                        act.activation(lo[:, i % 2, 1], lo[:, i % 2, 1], ACT.Exp, scale=-1.0).then_inc(s_e, 1)

                def stage_b(i):
                    for n in range(NB):
                        act.wait_ge(s_t, (i - 1) * NB + n + 1)
                        act.copy(turned[:, n].rearrange("p h t -> p (h t)"), k.ps[0:DK, 3 + n % 4, :]).then_inc(s_tk, 1)
                    act.wait_ge(s_o, i)
                    act.copy(k.cat[:, i, 0:W], k.ps[:, 5, :]).then_inc(s_ok, 1)

                stage_a(0)
                for i in range(TILES):
                    if i + 1 < TILES:
                        stage_a(i + 1)
                    if i:
                        stage_b(i)

            @block.vector
            def _(dve):
                def stage_a(i):
                    rows = META if i == 0 else P
                    qk = k.meta_qk[:] if i == 0 else k.qk[:, i, :]
                    dve.wait_ge(s_c, i + 1)
                    if i >= 2:
                        dve.wait_ge(s_t, (i - 2) * NB)
                    if i:
                        exps = flat[:, 0:LV * GW]
                        dve.tensor_scalar(lo[:, i % 2, 0].rearrange("p l n -> p (l n)"), exps, CLAMP, None, ALU.min).then_inc(s_clip, 1)
                        dve.tensor_scalar(lo[:, i % 2, 1].rearrange("p l n -> p (l n)"), exps, -CLAMP, None, ALU.max).then_inc(s_clip, 1)
                        dve.wait_ge(s_e, 3 * i)
                        q3 = qk[:, 0:GW].unsqueeze(1).to_broadcast([P, LV, GW])
                        k3 = qk[:, GW:2 * GW].unsqueeze(1).to_broadcast([P, LV, GW])
                        dve.scalar_tensor_tensor(out=lo[:, i % 2, 0], in0=lo[:, i % 2, 0], scalar=DK ** -0.5, in1=q3, op0=ALU.mult, op1=ALU.mult)
                        dve.scalar_tensor_tensor(out=q_st[:, i % 2], in0=end[:, 0, :], scalar=DK ** -0.5, in1=qk[:, 0:GW],
                                                 op0=ALU.mult, op1=ALU.mult)
                        dve.tensor_tensor(lo[:, i % 2, 1], lo[:, i % 2, 1], k3, ALU.mult)
                    dve.wait_ge(s_d, i + 1)
                    if i >= 2:
                        dve.wait_ge(s_k, i - 1)
                    dve.tensor_tensor(k_st[0:rows, i % 2, :], end[0:rows, 1, :], qk[:, GW:2 * GW], ALU.mult).then_inc(s_q, 1)

                def stage_b(i):
                    dve.wait_ge(s_k, i + 1)
                    new = k.ps[0:DK, 7, :].rearrange("p (h n) -> p h n", h=HEADS)
                    if i:
                        if i >= 2:
                            dve.wait_ge(s_o, i - 1)
                        dve.wait_ge(s_s, i)
                        dve.tensor_tensor(states[i % 2], states[(i - 1) % 2], last[:, i % 2, :].unsqueeze(2).to_broadcast([DK, HEADS, DV]),
                                          ALU.mult).then_inc(s_sch, 1)
                        dve.wait_ge(s_sch, i)
                        dve.tensor_tensor(states[i % 2], states[i % 2], new, ALU.add).then_inc(s_s, 1)
                    else:
                        dve.tensor_copy(states[0], new).then_inc(s_s, 1)
                    for n in range(LV) if i else ():
                        dve.wait_ge(s_a, (i - 1) * LV + n + 1)
                        if n == 0 and i >= 2:
                            dve.wait_ge(s_o, i - 1)
                        dve.tensor_tensor(pairs[:, n], k.ps[:, 3 + (n + 3) % 4, :].rearrange("p (h t) -> p h t", h=HEADS),
                                          const(k, f"pair{n}").unsqueeze(1).to_broadcast([P, HEADS, P]), ALU.mult).then_inc(s_m, 1)

                stage_a(0)
                for i in range(TILES):
                    if i + 1 < TILES:
                        stage_a(i + 1)
                    stage_b(i)

            @block.gpsimd
            def _(pool):
                pool.memset(zeros, 0.0).then_inc(s_zero, 1)

            @block.sync
            def _(sp):
                for half in range(2):
                    a, b = 1 + 4 * half, 5 + 4 * half
                    sp.dma_start(k.v[:, a:b], k.v_d[a:b].rearrange("i p n -> p i n")).then_inc(s_v[half], 16)
                rows = io["v_prompt"].rearrange("a n l h d -> (a n) (l h d)")[META:META + SEQ]
                sp.dma_start(k.dv[:, 1:TILES], rows.rearrange("(i p) n -> p i n", p=P)).then_inc(s_dv, 16)
                sp.wait_ge(s_dv, 16)
                sp.wait_ge(s_zero, 1)
                spare = k.ys[EXPERTS * BLOCK:(EXPERTS + SPARE) * BLOCK].rearrange("(p b) (j n) -> p (b j) n", p=P, n=W)
                sp.dma_start(spare, zeros.unsqueeze(1).to_broadcast([P, SPARE * (D // W), W])).then_inc(s_spare, 16)
                sp.wait_ge(s_spare, 16)
                sp.wait_ge(s_s, TILES)
                sp.dma_start(io["gla_prompt"][0, 0].rearrange("h k v -> k h v"), states[(TILES - 1) % 2]).then_inc(s_out, 16)
                sp.wait_ge(s_out, 16)




def sample_linear_attention(nc, k, io):
    with ExitStack() as ctx:
        def sb(name, shape, dt=F32):
            return ctx.enter_context(nc.sbuf_tensor(name, shape, dt))

        sem = k.sem
        old = sb("h_old", [DK, SAMPLES, HEADS, DV])
        lo = sb("h_lo", [NS, 4, GW])
        qk = sb("h_qk", [NS, 4, GW])
        km = sb("h_km", [NS, SAMPLES, GW])
        turned = sb("h_turned", [DK, 3, HEADS, NS])
        pairs = sb("h_pairs", [NS, HEADS, NS])
        qm = sb("h_qm", [DK, HEADS, SAMPLES, NS])
        last = sb("h_last", [DK, HEADS, SAMPLES])
        s_old, s_c, s_clip, s_e, s_d, s_q, s_t, s_tk = (sem("h_old"), sem("h_c"), sem("h_clip"), sem("h_e"), sem("h_d"),
                                                        sem("h_q"), sem("h_t"), sem("h_tk"))
        s_a, s_m, s_o, s_k, s_new, s_out = sem("h_a"), sem("h_m"), sem("h_o"), sem("h_k"), sem("h_new"), sem("h_out")
        s_dec, s_qm, s_qmz = sem("h_dec"), sem("h_qm_"), sem("h_qmz")
        flat = k.ps[:].rearrange("p b n -> p (b n)")
        z, v = k.z[0:NS, 0, :], k.sample_v[:]

        with nc.Block() as block:
            @block.sync
            def _(sp):
                sp.dma_start(old[:], io["state_gla"][:, 0].rearrange("b h k v -> k b h v")).then_inc(s_old, 16)
                for b in range(SAMPLES):
                    sp.wait_ge(s_new, b + 1)
                    sp.dma_start(io["gla_sample"][b, 0].rearrange("h k v -> k h v"), old[:, b]).then_inc(s_out, 16)
                sp.wait_ge(s_out, 16 * SAMPLES)

            @block.gpsimd
            def _(pool):
                pool.memset(qm[:], 0.0).then_inc(s_qmz, 1)

            @block.tensor
            def _(pe):
                ident = const(k, "ident")
                for n, name in enumerate(("s_rel", "s_cum", "s_rest")):
                    pe.matmul(flat[0:NS, n * GW:(n + 1) * GW], const(k, name, NS), z, start=True, stop=True)
                for h in range(HEADS):
                    mm = pe.matmul(k.ps[0:DK, 2, h * SAMPLES:(h + 1) * SAMPLES], z[:, h * DK:(h + 1) * DK], const(k, "s_tau", NS),
                                   start=True, stop=True)
                mm.then_inc(s_c, 1)
                pe.wait_ge(s_q, 1)
                for n in range(3):
                    for h in range(HEADS):
                        m = n * HEADS + h
                        mm = pe.transpose(k.ps[0:DK, 3, m * NS:(m + 1) * NS], qk[:, n, h * DK:(h + 1) * DK], ident[0:NS, 0:NS])
                mm.then_inc(s_t, 1)
                pe.wait_ge(s_tk, 1)
                for h in range(HEADS):
                    mm = pe.matmul(k.ps[0:NS, 4, h * NS:(h + 1) * NS], turned[:, 1, h, :], turned[:, 0, h, :], start=True, stop=True)
                mm.then_inc(s_a, 1)
                pe.wait_ge(s_m, 1)
                pe.wait_ge(s_old, 16)
                pe.wait_ge(s_qm, 1)
                for h in range(HEADS):
                    out = k.ps[0:NS, 5, h * DV:(h + 1) * DV]
                    pe.matmul(out, pairs[:, h, :], v[:, h * DV:(h + 1) * DV], start=True, stop=False)
                    for b in range(SAMPLES):
                        mm = pe.matmul(out, qm[:, h, b, :], old[:, b, h, :], start=False, stop=b == SAMPLES - 1)
                mm.then_inc(s_o, 1)
                for b in range(SAMPLES):
                    if b >= 4:
                        pe.wait_ge(s_new, b - 3)
                    for h in range(HEADS):
                        mm = pe.matmul(k.ps[0:DK, b % 4, h * DV:(h + 1) * DV], km[:, b, h * DK:(h + 1) * DK], v[:, h * DV:(h + 1) * DV],
                                       start=True, stop=True)
                    mm.then_inc(s_k, 1)

            @block.scalar
            def _(act):
                act.wait_ge(s_clip, 2)
                act.activation(lo[:, 0], lo[:, 0], ACT.Exp).then_inc(s_e, 1)
                act.activation(lo[:, 1], lo[:, 1], ACT.Exp, scale=-1.0).then_inc(s_e, 1)
                act.activation(lo[:, 2], flat[0:NS, GW:2 * GW], ACT.Exp).then_inc(s_e, 1)
                act.activation(lo[:, 3], flat[0:NS, 2 * GW:3 * GW], ACT.Exp).then_inc(s_e, 1)
                act.activation(last[:].rearrange("p h b -> p (h b)"), k.ps[0:DK, 2, 0:HEADS * SAMPLES], ACT.Exp).then_inc(s_e, 1)
                act.wait_ge(s_o, 1)
                act.copy(k.cat[0:NS, 0, 0:W], k.ps[0:NS, 5, :])

            @block.vector
            def _(dve):
                dve.wait_ge(s_c, 1)
                dve.tensor_scalar(lo[:, 0], flat[0:NS, 0:GW], CLAMP, None, ALU.min).then_inc(s_clip, 1)
                dve.tensor_scalar(lo[:, 1], flat[0:NS, 0:GW], -CLAMP, None, ALU.max).then_inc(s_clip, 1)
                dve.wait_ge(s_e, 5)
                q, kk = k.qk[0:NS, 0, 0:GW], k.qk[0:NS, 0, GW:2 * GW]
                dve.scalar_tensor_tensor(out=qk[:, 0], in0=lo[:, 0], scalar=DK ** -0.5, in1=q, op0=ALU.mult, op1=ALU.mult)
                dve.tensor_tensor(qk[:, 1], lo[:, 1], kk, ALU.mult)
                dve.scalar_tensor_tensor(out=qk[:, 2], in0=lo[:, 2], scalar=DK ** -0.5, in1=q, op0=ALU.mult, op1=ALU.mult).then_inc(s_q, 1)
                dve.tensor_tensor(qk[:, 3], lo[:, 3], kk, ALU.mult).then_inc(s_d, 1)
                dve.wait_ge(s_t, 1)
                dve.tensor_copy(turned[:].rearrange("p n h t -> p (n h t)"), k.ps[0:DK, 3, 0:3 * HEADS * NS]).then_inc(s_tk, 1)
                dve.wait_ge(s_tk, 1)
                dve.wait_ge(s_qmz, 1)
                for b in range(SAMPLES):
                    t = slice(b * STEPS, (b + 1) * STEPS)
                    ins = dve.tensor_copy(qm[:, :, b, t], turned[:, 2, :, t])
                ins.then_inc(s_qm, 1)
                dve.wait_ge(s_d, 1)
                dve.tensor_tensor(km[:], qk[:, 3].unsqueeze(1).to_broadcast([NS, SAMPLES, GW]),
                                  const(k, "s_of", NS).unsqueeze(2).to_broadcast([NS, SAMPLES, GW]), ALU.mult)
                dve.wait_ge(s_a, 1)
                dve.tensor_tensor(pairs[:], k.ps[0:NS, 4, 0:HEADS * NS].rearrange("p (h t) -> p h t", h=HEADS),
                                  const(k, "s_pair", NS).unsqueeze(1).to_broadcast([NS, HEADS, NS]), ALU.mult).then_inc(s_m, 1)
                dve.wait_ge(s_o, 1)
                for b in range(SAMPLES):
                    dve.tensor_tensor(old[:, b], old[:, b], last[:, :, b].unsqueeze(2).to_broadcast([DK, HEADS, DV]), ALU.mult).then_inc(s_dec, 1)
                for b in range(SAMPLES):
                    dve.wait_ge(s_k, b + 1)
                    dve.wait_ge(s_dec, b + 1)
                    dve.tensor_tensor(old[:, b], old[:, b], k.ps[0:DK, b % 4, :].rearrange("p (h n) -> p h n", h=HEADS), ALU.add).then_inc(s_new, 1)




def prompt_attention(nc, k, io):
    with ExitStack() as ctx:
        def sb(name, shape, dt=F32):
            return ctx.enter_context(nc.sbuf_tensor(name, shape, dt))

        sem = k.sem
        probs = sb("a_probs", [P, 2, 2, META + SEQ])
        turned = sb("a_turned", [P, 2, 4, P])
        m = sb("a_m", [P, 8, 8])
        meta_m = sb("a_meta_m", [P, 2, 8])
        lam4 = sb("a_lam4", [P, 4, DK])
        lamp = sb("a_lamp", [P, 2, DK])
        lams = sb("a_lams", [P, 2])
        s_lam, s_lamd, s_lame, s_ch = sem("a_lam"), sem("a_lamd"), sem("a_lame"), sem("a_ch")
        s_ms, s_mm, s_s, s_max, s_exp, s_p, s_t, s_tk = (sem("a_ms"), sem("a_mm"), sem("a_s"), sem("a_max"), sem("a_exp"),
                                                         sem("a_p"), sem("a_t"), sem("a_tk"))
        s_o, s_ok, s_lamb = sem("a_o"), sem("a_ok"), sem("a_lamb")
        STEP = [(i, h) for i in range(1, TILES) for h in range(HEADS)]
        GROUPS_OF = {i: [list(range(0, i + 1))[a:a + 4] for a in range(0, i + 1, 4)] for i in range(1, TILES)}
        start, total = [], 0
        for i, h in STEP:
            start.append(total)
            total += len(GROUPS_OF[i])
        scale = DK ** -0.5

        with nc.Block() as block:
            @block.sync
            def _(sp):
                for n, name in enumerate(("lam_q1", "lam_k1", "lam_q2", "lam_k2")):
                    sp.dma_start(lam4[:, n, :], io[name].to_broadcast([P, DK])).then_inc(s_lam, 16)

            @block.tensor
            def _(pe):
                ident = const(k, "ident")

                def scores(n):
                    i, h = STEP[n]
                    if h == 0:
                        if i >= 2:
                            pe.wait_ge(s_exp, 8 * (i - 1))
                        for c in range(2):
                            for g in range(HEADS):
                                a = META * (2 * g + c)
                                mm = pe.matmul(k.ps[:, 4, a:a + META], k.qT[64 * c:64 * c + 64, g, P * (i - 1):P * i],
                                               k.meta_kT[64 * c:64 * c + 64, g, :], start=True, stop=True)
                            mm.then_inc(s_ms, 1)
                            if c == 0:
                                pe.wait_ge(s_ms, 2 * i - 1)
                    for a in range(0, P * i, 512):
                        b = min(a + 512, P * i)
                        for c in range(2):
                            if n and a == 0:
                                pe.wait_ge(s_exp, 2 * (n - 1) + c + 1)
                            mm = pe.matmul(k.ps[:, 2 * c + a // 512, 0:b - a], k.qT[64 * c:64 * c + 64, h, P * (i - 1):P * i],
                                           k.kT[64 * c:64 * c + 64, h, a:b], start=True, stop=True)
                            if b == P * i:
                                mm.then_inc(s_s, 1)

                def outputs(n):
                    i, h = STEP[n]
                    out = k.ps[:, 7, h * DV:(h + 1) * DV]
                    pe.wait_ge(s_p, n + 1)
                    if h == 0 and i >= 2:
                        pe.wait_ge(s_ok, i - 1)

                    def turn(j):
                        g = start[n] + j
                        if g >= 2:
                            pe.wait_ge(s_tk, g - 1)
                        for x, blk in enumerate(GROUPS_OF[i][j]):
                            a, w = (0, META) if blk == 0 else (META + P * (blk - 1), P)
                            mm = pe.transpose(k.ps[0:w, 5 + g % 2, x * P:(x + 1) * P], probs[:, n % 2, 0, a:a + w], ident)
                        mm.then_inc(s_t, 1)

                    turn(0)
                    for j, blocks in enumerate(GROUPS_OF[i]):
                        if j + 1 < len(GROUPS_OF[i]):
                            turn(j + 1)
                        g = start[n] + j
                        pe.wait_ge(s_tk, g + 1)
                        for x, blk in enumerate(blocks):
                            w = META if blk == 0 else P
                            v = k.meta_dv[:] if blk == 0 else k.dv[:, blk, :]
                            mm = pe.matmul(out, turned[0:w, g % 2, x, :], v[:, h * DV:(h + 1) * DV], start=blk == 0, stop=blk == i)
                    mm.then_inc(s_o, 1)

                for n in range(len(STEP) + 1):
                    if n < len(STEP):
                        scores(n)
                    if n:
                        outputs(n - 1)

            @block.scalar
            def _(act):
                act.wait_ge(s_lamd, 2)
                act.activation(lams[:], lams[:], ACT.Exp).then_inc(s_lame, 1)

                def exponentials(n, c):
                    i, h = STEP[n]
                    x = 2 * h + c
                    act.wait_ge(s_max, 2 * n + c + 1)
                    if n >= 2:
                        act.wait_ge(s_t, start[n - 1])
                    act.activation(probs[:, n % 2, c, 0:META], k.ps[:, 4, META * x:META * (x + 1)], ACT.Exp, scale=scale,
                                   bias=m[:, 1, x:x + 1], accum_out=m[:, 2, x:x + 1])
                    act.activation(probs[:, n % 2, c, META:META + P * i],
                                   k.ps[:, 2 * c:2 * c + 2, :].rearrange("p b n -> p (b n)")[:, 0:P * i], ACT.Exp, scale=scale,
                                   bias=m[:, 1, x:x + 1], accum_out=m[:, 3, x:x + 1]).then_inc(s_exp, 1)

                def keep(n, j):
                    g, blocks = start[n] + j, GROUPS_OF[STEP[n][0]][j]
                    act.wait_ge(s_t, g + 1)
                    first = 1 if blocks[0] == 0 else 0
                    if first:
                        act.copy(turned[0:META, g % 2, 0, :], k.ps[0:META, 5 + g % 2, 0:P])
                    b = len(blocks)
                    act.copy(turned[:, g % 2, first:b, :].rearrange("p x t -> p (x t)"), k.ps[:, 5 + g % 2, first * P:b * P]).then_inc(s_tk, 1)

                for n in range(len(STEP) + 1):
                    if n:
                        keep(n - 1, 0)
                    if n < len(STEP):
                        exponentials(n, 0)
                    if n and len(GROUPS_OF[STEP[n - 1][0]]) > 1:
                        keep(n - 1, 1)
                    if n < len(STEP):
                        exponentials(n, 1)
                    if n:
                        i, h = STEP[n - 1]
                        for j in range(2, len(GROUPS_OF[i])):
                            keep(n - 1, j)
                        if h == HEADS - 1:
                            act.wait_ge(s_o, n)
                            act.copy(k.cat[:, i, W:D], k.ps[:, 7, :]).then_inc(s_ok, 1)

            @block.vector
            def _(dve):
                chain = Chain(dve, s_ch)
                dve.wait_ge(s_lam, 64)
                for n in range(2):
                    dve.tensor_tensor_reduce(lamp[:, n, :], lam4[:, 2 * n, :], lam4[:, 2 * n + 1, :], 1.0, 0.0, ALU.mult, ALU.add,
                                             lams[:, n:n + 1]).then_inc(s_lamd, 1)
                dve.wait_ge(s_lame, 1)
                dve.scalar_tensor_tensor(out=k.neg_lam[:], in0=lams[:, 1:2], scalar=-LAM_INIT, in1=lams[:, 0:1], op0=ALU.add,
                                         op1=ALU.subtract).then_inc(s_lamb, 1)
                dve.wait_ge(s_lamb, 1)

                def maxima(n):
                    i, h = STEP[n]
                    if h == 0:
                        dve.wait_ge(s_ms, 2 * i)
                        dve.reduce_max(meta_m[:, i % 2, :], k.ps[:, 4, 0:8 * META].rearrange("p (x j) -> p x j", x=8), axis=X).then_inc(s_mm, 1)
                    for c in range(2):
                        x = 2 * h + c
                        s = k.ps[:, 2 * c:2 * c + 2, :].rearrange("p b n -> p (b n)")
                        dve.wait_ge(s_s, 2 * n + c + 1)
                        diag = s[:, P * (i - 1):P * i]
                        chain.link(dve.tensor_tensor(diag, diag, const(k, "causal"), ALU.add))
                        chain.link(dve.reduce_max(m[:, 0, x:x + 1], s[:, 0:P * i], axis=X))
                        dve.wait_ge(s_mm, i)
                        dve.tensor_scalar(m[:, 1, x:x + 1], m[:, 0, x:x + 1], meta_m[:, i % 2, x:x + 1], -scale, ALU.max, ALU.mult).then_inc(s_max, 1)

                def combine(n):
                    i, h = STEP[n]
                    two = slice(2 * h, 2 * h + 2)
                    dve.wait_ge(s_exp, 2 * n + 2)
                    chain.link(dve.tensor_tensor(m[:, 4, two], m[:, 2, two], m[:, 3, two], ALU.add))
                    chain.link(dve.reciprocal(m[:, 5, two], m[:, 4, two]))
                    chain.link(dve.tensor_tensor(m[:, 6, 2 * h:2 * h + 1], m[:, 5, 2 * h + 1:2 * h + 2], k.neg_lam[:], ALU.mult))
                    p0, p1 = probs[:, n % 2, 0, 0:META + P * i], probs[:, n % 2, 1, 0:META + P * i]
                    chain.link(dve.tensor_scalar(p0, p0, m[:, 5, 2 * h:2 * h + 1], None, ALU.mult))
                    dve.scalar_tensor_tensor(out=p0, in0=p1, scalar=m[:, 6, 2 * h:2 * h + 1], in1=p0, op0=ALU.mult, op1=ALU.add).then_inc(s_p, 1)

                for n in range(len(STEP)):
                    maxima(n)
                    combine(n)




def sample_attention(nc, k, io):
    RING = 8
    PAST = PAGES * PAGE
    with ExitStack() as ctx:
        def sb(name, shape, dt=F32):
            return ctx.enter_context(nc.sbuf_tensor(name, shape, dt))

        sem = k.sem
        ring = sb("d_ring", [P, RING, GROUP, W])
        table = sb("d_table", [P, SAMPLES, PAGES], I32)
        rows_f = sb("d_rows_f", [P, SAMPLES, GROUPS])
        rows = sb("d_rows", [P, SAMPLES, GROUPS], I32)
        row = sb("d_row", [P, 2, GROUPS], U32)
        q = sb("d_q", [P, HEADS, 32])
        q_pad = sb("d_q_pad", [P, SAMPLES, HEADS, 32])
        kT = sb("d_kT", [P, 2, HEADS, 512])
        s = sb("d_s", [P, PAST + NS])
        top = sb("d_top", [P, GROUPS + 1])
        sums = sb("d_sums", [P, GROUPS + 1])
        m = sb("d_m", [P, 4])
        pT = sb("d_pT", [P, 2, GROUP, HEADS, 8])
        zeros = sb("d_zeros", [P, P])
        o = sb("d_o", [P, SAMPLES, DV])
        o2 = sb("d_o2", [NS, 2, W])
        bounce = nc.dram_tensor("d_bounce", (SAMPLES, STEPS, 2, HEADS, DV), F32, kind="Internal").ap()
        s_small = sem("d_small")
        s_tab, s_rowf, s_rows, s_row = sem("d_tab"), sem("d_rowf"), sem("d_rows_"), sem("d_row_")
        s_load = [sem(f"d_load{j}") for j in range(RING)]
        s_used, s_t, s_kta, s_ktd, s_qk, s_sc = (sem("d_used"), sem("d_t"), sem("d_kta"), sem("d_ktd"), sem("d_qk"),
                                                 sem("d_sc"))
        s_q, s_qkn, s_nm, s_exp, s_pt, s_ptk, s_pv = (sem("d_q_"), sem("d_qkn"), sem("d_nm"), sem("d_exp"), sem("d_pt"),
                                                      sem("d_ptk"), sem("d_pv"))
        s_o, s_ok, s_z, s_ch, s_pool, s_b, s_back = (sem("d_o_"), sem("d_ok"), sem("d_z"), sem("d_ch"), sem("d_pool"),
                                                     sem("d_b"), sem("d_back"))
        caches = [io[n].rearrange("n (a r) l h d -> (n a) (r l h d)", r=GROUP) for n in ("cache_k", "cache_v")]
        NX = GROUPS + 1
        PER = 2 * GROUPS
        scale = DK ** -0.5

        with nc.Block() as block:
            @block.sync
            def _(sp):
                sp.dma_start(table[:], io["page_table"].unsqueeze(0).to_broadcast([P, SAMPLES, PAGES])).then_inc(s_tab, 16)
                for n, name in enumerate(("gla_norm", "diff_norm")):
                    sp.dma_start(k.head_gain[:, n:n + 1], io[name].rearrange("a p -> p a")).then_inc(s_small, 16)
                sp.dma_start(k.gain2[:], io["norm2"].to_broadcast([P, D])).then_inc(s_small, 16)
                sp.dma_start(k.wr[:, :, 0:NGROUPS], io["w_route_group"][0].rearrange("(p k) n -> p k n", k=KD)).then_inc(s_small, 16)
                sp.dma_start(k.wr[:, :, NGROUPS:NR], io["w_route_expert"][0].rearrange("(p k) n -> p k n", k=KD)).then_inc(s_small, 16)
                sp.dma_start(k.br[:, 0:NGROUPS], io["b_route_group"].to_broadcast([P, NGROUPS])).then_inc(s_small, 16)
                sp.dma_start(k.br[:, NGROUPS:NR], io["b_route_expert"].to_broadcast([P, EXPERTS])).then_inc(s_small, 16)
                sp.wait_ge(s_ok, 1 + SAMPLES)
                for h in range(HEADS):
                    for c in range(2):
                        a = 32 * h + STEPS * c
                        sp.dma_start(bounce[:, :, c, h, :].rearrange("b t v -> t b v"), o[a:a + STEPS]).then_inc(s_b, 16)
                sp.wait_ge(s_b, 16 * 2 * HEADS)
                sp.dma_start(o2[:].rearrange("p c n -> p (c n)"), bounce.rearrange("b t c h v -> (b t) (c h v)")).then_inc(s_back, 16)
                sp.wait_ge(s_small, 16 * 7)

            @block.gpsimd
            def _(pool):
                pool.sem_inc(s_used, RING)
                pool.wait_ge(s_rows, 1)
                with pool.Fori(0, SAMPLES // 2) as pair:
                    for half in range(2):
                        b = pair * 2 + half
                        pool.wait_ge(s_used, pair * (2 * PER) + half * PER + 1)
                        pool.tensor_copy(row[:, half, :], rows[:, bass.ds(b, 1), :].rearrange("p a g -> p (a g)").bitcast(U32)).then_inc(s_row, 1)
                        pool.wait_ge(s_row, b + 1)
                        for x in range(PER):
                            pool.wait_ge(s_used, pair * (2 * PER) + (half * PER + x + 1))
                            pool.sem_inc(s_pool, 1)
                            pool.indirect_dma_start(out=ring[:, x % RING].rearrange("p r n -> p (r n)"), out_offset=None,
                                                    in_=caches[x // GROUPS],
                                                    in_offset=bass.IndirectOffsetOnAxis(ap=row[:, half, x % GROUPS:x % GROUPS + 1], axis=0)
                                                    ).then_inc(s_load[x % RING], 16)

            def arrived(eng, b, x):
                eng.wait_ge(s_load[x % RING], b * (16 * PER // RING) + 16 * (x // RING + 1))

            @block.tensor
            def _(pe):
                ident = const(k, "ident")
                pe.wait_ge(s_z, 1)
                with pe.Fori(0, SAMPLES) as b:
                    def turn(g):
                        arrived(pe, b, g)
                        for h in range(HEADS):
                            pe.wait_ge(s_ktd if h % 2 else s_kta, b * (2 * GROUPS) + (2 * g + h // 2 + 1))
                            if g == 0 and h == HEADS - 1:
                                pe.wait_ge(s_ok, b + 1)
                            for r in range(GROUP):
                                mm = pe.transpose(k.ps[:, h, r * P:(r + 1) * P], ring[:, g % RING, r, h * P:(h + 1) * P], ident)
                            mm.then_inc(s_t, 1)
                        pe.wait_ge(s_t, b * (4 * GROUPS) + 4 * (g + 1))
                        pe.sem_inc(s_used, 1)

                    def scores(g):
                        pe.wait_ge(s_kta, b * (2 * GROUPS) + (2 * g + 4))
                        pe.wait_ge(s_ktd, b * (2 * GROUPS) + (2 * g + 4))
                        pe.wait_ge(s_sc, b * GROUPS + (g + 1))
                        for h in range(HEADS):
                            mm = pe.matmul(k.ps[32 * h:32 * h + 32, 4 + g % 2, :], q[:, h, :], kT[:, g % 2, h, :], start=True, stop=True)
                        mm.then_inc(s_qk, 1)

                    pe.wait_ge(s_q, b + 1)
                    pe.wait_ge(s_ptk, b * NX + 2)
                    for h in range(HEADS):
                        mm = pe.matmul(k.ps[32 * h:32 * h + 32, 6, 0:NS], q[:, h, :], k.kTs[:, h, :], start=True, stop=True)
                    mm.then_inc(s_qkn, 1)
                    for g in range(GROUPS + 1):
                        if g < GROUPS:
                            turn(g)
                        if g:
                            scores(g - 1)

                    def turn_probs(x):
                        pe.wait_ge(s_exp, b * NX + (x + 1))
                        pe.wait_ge(s_ptk, b * NX + max(x + 1, 2) + (1 if x == 1 else 0))
                        bank = k.ps[:, 6 + x % 2, :]
                        if x == 0:
                            mm = pe.transpose(bank[0:NS, 0:P], s[:, PAST:PAST + NS], ident)
                        else:
                            for r in range(GROUP):
                                a = 512 * (x - 1) + P * r
                                mm = pe.transpose(bank[:, r * P:(r + 1) * P], s[:, a:a + P], ident)
                        mm.then_inc(s_pt, 1)

                    turn_probs(0)
                    pe.matmul(k.ps[:, 3, 0:DV], zeros[:], ident, start=True, stop=False, skip_group_check=True)
                    for x in range(NX):
                        if x + 1 < NX:
                            turn_probs(x + 1)
                        if x:
                            pe.wait_ge(s_ptk, b * NX + (x + 3))
                            arrived(pe, b, GROUPS + x - 1)
                        last = x == NX - 1
                        for r in range(GROUP if x else 1):
                            for h in range(HEADS):
                                n = P if x else NS
                                v = ring[:, (GROUPS + x - 1) % RING, r, :] if x else k.new_v[:]
                                mm = pe.matmul(k.ps[32 * h:32 * h + 8, 3, 0:DV], pT[0:n, x % 2, r, h, :], v[:, h * DV:(h + 1) * DV],
                                               start=False, stop=last and r == GROUP - 1, skip_group_check=True)
                        mm.then_inc(s_pv, 1)
                        if x:
                            pe.wait_ge(s_pv, b * NX + (x + 3))
                            pe.sem_inc(s_used, 1)
                    pe.sem_inc(s_o, 1)

            @block.scalar
            def _(act):
                act.sem_inc(s_kta, 2)
                act.sem_inc(s_sc, 2)
                with act.Fori(0, SAMPLES) as b:
                    def keep(g, h):
                        act.wait_ge(s_t, b * (4 * GROUPS) + (4 * g + h + 1))
                        act.wait_ge(s_qk, b * GROUPS + (g + 1))
                        act.copy(kT[:, g % 2, h, :], k.ps[:, h, :]).then_inc(s_kta, 1)

                    def keep_scores(g):
                        act.wait_ge(s_qk, b * GROUPS + (g + 3))
                        act.copy(s[:, 512 * g:512 * (g + 1)], k.ps[:, 4 + g % 2, :]).then_inc(s_sc, 1)

                    for g in range(GROUPS):
                        keep(g, 0)
                        keep(g, 2)
                        if g:
                            keep_scores(g - 1)
                    keep_scores(GROUPS - 1)
                    act.wait_ge(s_nm, b + 1)
                    for x in range(NX):
                        a, n = (PAST, NS) if x == 0 else (512 * (x - 1), 512)
                        act.activation(s[:, a:a + n], s[:, a:a + n], ACT.Exp, scale=scale, bias=m[:, 1:2],
                                       accum_out=sums[:, x:x + 1]).then_inc(s_exp, 1)

            @block.vector
            def _(dve):
                chain = Chain(dve, s_ch)
                dve.memset(zeros[:], 0.0).then_inc(s_z, 1)
                chain.link(dve.memset(q_pad[:], 0.0))
                for c in range(2):
                    chain.link(dve.tensor_copy(q_pad[64 * c:64 * c + 64, :, :, STEPS * c:STEPS * c + STEPS],
                                               k.qTs[64 * c:64 * c + 64].rearrange("p h (b t) -> p b h t", t=STEPS)))
                dve.sem_inc(s_ktd, 2)
                dve.sem_inc(s_qk, 2)
                dve.sem_inc(s_ptk, 2)
                dve.sem_inc(s_pv, 2)
                dve.sem_inc(s_ok, 1)
                dve.wait_ge(s_tab, 16)
                for n in range(GROUP):
                    part = slice(32 * n, 32 * n + 32)
                    pages = table[part].rearrange("p b (g n) -> p b g n", n=GROUP)[:, :, :, n]
                    dve.tensor_scalar(rows_f[part], pages, float(PAGE // GROUP), const(k, "in_page")[part], ALU.mult, ALU.add).then_inc(s_rowf, 1)
                dve.wait_ge(s_rowf, GROUP)
                dve.tensor_copy(rows[:], rows_f[:]).then_inc(s_rows, 1)
                with dve.Fori(0, SAMPLES) as b:
                    chain.loop(b, 5)
                    dve.tensor_copy(q[:], q_pad[:, bass.ds(b, 1)].rearrange("p a h x -> p (a h) x")).then_inc(s_q, 1)

                    def keep(g, h):
                        dve.wait_ge(s_t, b * (4 * GROUPS) + (4 * g + h + 1))
                        dve.wait_ge(s_qk, b * GROUPS + (g + 1))
                        dve.tensor_copy(kT[:, g % 2, h, :], k.ps[:, h, :]).then_inc(s_ktd, 1)

                    def maximum(g):
                        dve.wait_ge(s_sc, b * GROUPS + (g + 3))
                        return dve.reduce_max(top[:, g:g + 1], s[:, 512 * g:512 * (g + 1)], axis=X)

                    dve.wait_ge(s_qkn, b + 1)
                    mask = const(k, "new_mask")[:, bass.ds(b * NS, NS)]
                    chain.link(dve.tensor_tensor(s[:, PAST:PAST + NS], k.ps[:, 6, 0:NS], mask, ALU.add))
                    dve.reduce_max(top[:, GROUPS:GROUPS + 1], s[:, PAST:PAST + NS], axis=X)
                    for g in range(GROUPS):
                        keep(g, 1)
                        keep(g, 3)
                        if g:
                            maximum(g - 1)
                    chain.link(maximum(GROUPS - 1))
                    chain.link(dve.reduce_max(m[:, 0:1], top[:], axis=X))
                    dve.tensor_scalar(m[:, 1:2], m[:, 0:1], -scale, None, ALU.mult).then_inc(s_nm, 1)
                    for x in range(NX):
                        dve.wait_ge(s_pt, b * NX + (x + 1))
                        dve.wait_ge(s_pv, b * NX + (x + 1))
                        bank = k.ps[:, 6 + x % 2, :].rearrange("p (r h j) -> p r h j", r=GROUP, h=HEADS)
                        if x == 0:
                            dve.tensor_copy(pT[0:NS, 0, 0], bank[0:NS, 0, :, 0:8]).then_inc(s_ptk, 1)
                        else:
                            dve.tensor_copy(pT[:, x % 2], bank[:, :, :, 0:8]).then_inc(s_ptk, 1)
                    dve.wait_ge(s_exp, b * NX + NX)
                    chain.link(dve.reduce_sum(m[:, 2:3], sums[:], axis=X))
                    chain.link(dve.reciprocal(m[:, 3:4], m[:, 2:3]))
                    dve.wait_ge(s_o, b + 1)
                    dve.tensor_scalar(o[:, bass.ds(b, 1), :].rearrange("p a v -> p (a v)"), k.ps[:, 3, 0:DV], m[:, 3:4], None, ALU.mult).then_inc(s_ok, 1)
                chain.end(SAMPLES)
                dve.wait_ge(s_back, 16)
                dve.scalar_tensor_tensor(out=k.cat[0:NS, 0, W:D], in0=o2[:, 1, :], scalar=k.neg_lam[0:NS], in1=o2[:, 0, :], op0=ALU.mult,
                                         op1=ALU.add)




def merge_and_route(nc, k, io):
    with ExitStack() as ctx:
        def sb(name, shape, dt=F32):
            return ctx.enter_context(nc.sbuf_tensor(name, shape, dt))

        sem = k.sem
        gate = sb("m_gate", [P, TILES, W])
        wout = sb("m_wout", [P, KD, D])
        wr, br, gain2, head_gain = k.wr, k.br, k.gain2, k.head_gain
        xres = sb("m_xres", [P, 2, D])
        sq = sb("m_sq", [P, D])
        r8 = sb("m_r8", [P, 8])
        r1 = sb("m_r1", [P, 2])
        catT = sb("m_catT", [P, 2, KD, P])
        xn = sb("m_xn", [P, 2, D])
        xnT = sb("m_xnT", [P, KD, P])
        lg = sb("m_lg", [P, TILES, NR])
        s_first, s_gate, s_silu = sem("m_first"), [sem("m_gate0"), sem("m_gate1")], sem("m_silu")
        s_w, s_x = [sem("m_w0"), sem("m_w1")], [sem("m_x0"), sem("m_x1")]
        s_sq, s_ms, s_rt, s_cat, s_t, s_tk, s_o, s_h = (sem("m_sq_"), sem("m_ms"), sem("m_rt"), sem("m_cat"), sem("m_t"),
                                                        sem("m_tk"), sem("m_o"), sem("m_h"))
        s_sq2, s_ms2, s_rt2, s_xn, s_t2, s_t2k, s_r, s_lg = (sem("m_sq2"), sem("m_ms2"), sem("m_rt2"), sem("m_xn_"),
                                                             sem("m_t2"), sem("m_t2k"), sem("m_r"), sem("m_lg_"))
        s_ch, s_st = sem("m_ch"), [sem("m_st0"), sem("m_st1")]
        x_rows = io["x_prompt"][0].rearrange("(i p) d -> i p d", p=P)

        def rows_of(i):
            return NS if i == 0 else P

        def dram_rows(t, i):
            return t[0:NS] if i == 0 else t[NS + P * (i - 1):NS + P * i]

        with nc.Block() as block:
            @block.sync
            def _(sp):
                sp.dma_start(gate[0:NS, 0, :], k.gate_d[0, 0:NS]).then_inc(s_gate[0], 16)
                for half in range(2):
                    part = slice(KD // 2 * half, KD // 2 * (half + 1))
                    sp.dma_start(wout[:, part], io["w_out"][0].rearrange("(k p) n -> p k n", p=P)[:, part]).then_inc(s_w[half], 16)
                sp.dma_start(gate[:, 1:TILES, :], k.gate_d[1:TILES].rearrange("i p n -> p i n")).then_inc(s_gate[1], 16)
                for i in range(TILES + 1):
                    if i < TILES:
                        if i >= 2:
                            sp.wait_ge(s_h, i - 1)
                        src = io["x_sample"].rearrange("b t d -> (b t) d") if i == 0 else x_rows[i - 1]
                        sp.dma_start(xres[0:rows_of(i), i % 2, :], src).then_inc(s_x[i % 2], 16)
                    if i == 3:
                        for t, name in ((k.first_w13[:, 0], "w_up"), (k.first_w13[:, 1], "w_gate"), (k.first_w2[:], "w_down")):
                            sp.dma_start(t, io[name][0, 0].rearrange("(p k) f -> p k f", p=P)).then_inc(s_first, 16)
                    if i:
                        j = i - 1
                        sp.wait_ge(s_xn, j + 1)
                        sp.dma_start(dram_rows(k.xn, j), xn[0:rows_of(j), j % 2, :]).then_inc(s_st[j % 2], 16)
                sp.wait_ge(s_first, 48)
                sp.wait_ge(s_st[0], 16 * 5)
                sp.wait_ge(s_st[1], 16 * 4)

            @block.tensor
            def _(pe):
                ident = const(k, "ident")

                def turn_heads(i):
                    n = rows_of(i)
                    pe.wait_ge(s_cat, i + 1)
                    if i:
                        pe.wait_ge(s_tk, 2 * i)
                    for half in range(2):
                        for j in range(4):
                            a = P * (4 * half + j)
                            mm = pe.transpose(k.ps[:, half, j * P:j * P + n], k.cat[0:n, i, a:a + P], ident[0:n, 0:n])
                        mm.then_inc(s_t, 1)

                def project_out(i):
                    n = rows_of(i)
                    pe.wait_ge(s_tk, 2 * i + 2)
                    if i:
                        pe.wait_ge(s_h, i)
                    for kk in range(KD):
                        if i == 0 and kk % (KD // 2) == 0:
                            pe.wait_ge(s_w[kk // (KD // 2)], 16)
                        for half in range(2):
                            mm = pe.matmul(k.ps[0:n, 2 + half, :], catT[:, i % 2, kk, 0:n], wout[:, kk, 512 * half:512 * (half + 1)],
                                           start=kk == 0, stop=kk == KD - 1)
                    mm.then_inc(s_o, 1)

                def turn_norm(i):
                    n = rows_of(i)
                    pe.wait_ge(s_xn, i + 1)
                    if i:
                        pe.wait_ge(s_t2k, 2 * i)
                    xk = xn[0:n, i % 2, :].rearrange("p (d k) -> p k d", k=KD)
                    for half in range(2):
                        for j in range(4):
                            mm = pe.transpose(k.ps[:, 4 + half, j * P:j * P + n], xk[:, 4 * half + j, :], ident[0:n, 0:n])
                        mm.then_inc(s_t2, 1)

                def route(i):
                    n = rows_of(i)
                    pe.wait_ge(s_t2k, 2 * i + 2)
                    if i:
                        pe.wait_ge(s_lg, i + 1)
                    for kk in range(KD):
                        mm = pe.matmul(k.ps[0:n, 6, 0:NR], xnT[:, kk, 0:n], wr[:, kk, :], start=kk == 0, stop=kk == KD - 1)
                    mm.then_inc(s_r, 1)

                for i in range(TILES + 3):
                    if 1 <= i <= TILES:
                        project_out(i - 1)
                    if i >= 3:
                        route(i - 3)
                    if i < TILES:
                        turn_heads(i)
                    if 2 <= i < TILES + 2:
                        turn_norm(i - 2)

            @block.scalar
            def _(act):

                def before(i):
                    n = rows_of(i)
                    act.activation(sq[0:n], k.cat[0:n, i, :], ACT.Square).then_inc(s_sq, 1)
                    act.wait_ge(s_ms, i + 1)
                    act.activation(r8[0:n], r8[0:n], ACT.Sqrt).then_inc(s_rt, 1)
                    for half in range(2):
                        act.wait_ge(s_t, 2 * i + half + 1)
                        if i >= 2:
                            act.wait_ge(s_o, i - 1)
                        act.activation(catT[:, i % 2, 4 * half:4 * half + 4, 0:n],
                                       k.ps[:, half, :].rearrange("p (j t) -> p j t", j=4)[:, :, 0:n], ACT.Copy,
                                       scale=head_gain[:, half:half + 1]).then_inc(s_tk, 1)

                def after(i):
                    n = rows_of(i)
                    act.wait_ge(s_h, i + 1)
                    act.activation(sq[0:n], k.h[0:n, i, :], ACT.Square, accum_out=r1[0:n, 0:1]).then_inc(s_sq2, 1)
                    act.wait_ge(s_ms2, i + 1)
                    act.activation(r1[0:n, 0:1], r1[0:n, 0:1], ACT.Sqrt).then_inc(s_rt2, 1)

                def keep_turned(i):
                    n = rows_of(i)
                    for half in range(2):
                        act.wait_ge(s_t2, 2 * i + half + 1)
                        act.copy(xnT[:, 4 * half:4 * half + 4, 0:n],
                                 k.ps[:, 4 + half, :].rearrange("p (j t) -> p j t", j=4)[:, :, 0:n]).then_inc(s_t2k, 1)

                def open_gates(n, g):
                    act.wait_ge(s_gate[n], 16)
                    act.activation(g, g, ACT.Silu).then_inc(s_silu, 1)

                open_gates(0, gate[0:NS, 0, :])
                act.wait_ge(s_ch, 1)
                for i in range(TILES + 2):
                    if i < TILES:
                        before(i)
                    if i == 0:
                        open_gates(1, gate[:, 1:TILES, :])
                    if i >= 2:
                        keep_turned(i - 2)
                    if 1 <= i <= TILES:
                        after(i - 1)

            @block.vector
            def _(dve):
                chain = Chain(dve, s_ch)
                chain.link(dve.tensor_scalar(head_gain[:, 1:2], head_gain[:, 1:2], 1.0 - LAM_INIT, None, ALU.mult))
                dve.memset(lg[:], 0.0).then_inc(s_lg, 1)

                def before(i):
                    n = rows_of(i)
                    dve.wait_ge(s_sq, i + 1)
                    if i:
                        dve.wait_ge(s_cat, i)
                    chain.link(dve.reduce_sum(r8[0:n], sq[0:n].rearrange("p (h v) -> p h v", h=8), axis=X))
                    dve.tensor_scalar(r8[0:n], r8[0:n], 1.0 / DV, EPS, ALU.mult, ALU.add).then_inc(s_ms, 1)
                    dve.wait_ge(s_rt, i + 1)
                    chain.link(dve.reciprocal(r8[0:n], r8[0:n]))
                    t = k.cat[0:n, i, :].rearrange("p (h v) -> p h v", h=8)
                    chain.link(dve.tensor_tensor(t, t, r8[0:n].unsqueeze(2).to_broadcast([n, 8, DV]), ALU.mult))
                    if i < 2:
                        dve.wait_ge(s_silu, i + 1)
                    t = k.cat[0:n, i, 0:W]
                    dve.tensor_tensor(t, t, gate[0:n, i, :], ALU.mult).then_inc(s_cat, 1)

                def after(i):
                    n = rows_of(i)
                    dve.wait_ge(s_o, i + 1)
                    dve.wait_ge(s_x[i % 2], 16 * (i // 2 + 1))
                    two = k.ps[0:n, 2:4, :].rearrange("p b n -> p (b n)")
                    dve.tensor_tensor(k.h[0:n, i, :], two, xres[0:n, i % 2, :], ALU.add).then_inc(s_h, 1)
                    dve.wait_ge(s_sq2, i + 1)
                    dve.tensor_scalar(r1[0:n, 0:1], r1[0:n, 0:1], 1.0 / D, EPS, ALU.mult, ALU.add).then_inc(s_ms2, 1)
                    dve.wait_ge(s_rt2, i + 1)
                    chain.link(dve.reciprocal(r1[0:n, 1:2], r1[0:n, 0:1]))
                    if i >= 2:
                        dve.wait_ge(s_t2, 2 * (i - 1))
                        dve.wait_ge(s_st[i % 2], 16 * (i // 2))
                    dve.scalar_tensor_tensor(out=xn[0:n, i % 2, :], in0=k.h[0:n, i, :], scalar=r1[0:n, 1:2], in1=gain2[0:n], op0=ALU.mult,
                                             op1=ALU.mult).then_inc(s_xn, 1)

                def logits(i):
                    n = rows_of(i)
                    dve.wait_ge(s_r, i + 1)
                    dve.tensor_tensor(lg[0:n, i, :], k.ps[0:n, 6, 0:NR], br[0:n], ALU.add).then_inc(s_lg, 1)

                for i in range(TILES + 3):
                    if i < TILES:
                        before(i)
                    if 1 <= i <= TILES:
                        after(i - 1)
                    if i >= 3:
                        logits(i - 3)

        T = TILES
        t4, t32, u32 = sb("r_t4", [P, T, NGROUPS]), sb("r_t32", [P, T, EXPERTS]), sb("r_u32", [P, T, EXPERTS])
        le = sb("r_le", [P, T, EXPERTS])
        one1, one2, both, prefix = (sb("r_one1", [P, T, EXPERTS]), sb("r_one2", [P, T, EXPERTS]), sb("r_both", [P, T, EXPERTS]),
                                    sb("r_prefix", [P, T, EXPERTS]))
        c = sb("r_c", [P, 12, T])
        e32 = sb("r_e32", [P, 6, EXPERTS])
        ei = sb("r_ei", [P, EXPERTS], I32)
        ci = sb("r_ci", [P, T], I32)
        spare_f = sb("r_spare_f", [1, SPARE, EXPERTS])
        zero = sb("r_zero", [(EXPERTS + SPARE), BLOCK])
        order_f = sb("r_order_f", [EXPERTS + SPARE, BLOCK])
        q_ch, q_exp, q_ex, q_both, q_rank, q_cnt, q_zero, q_zd, q_sl, q_sc, q_ord, q_ot = (
            sem("q_ch"), sem("q_exp"), sem("q_ex"), sem("q_both"), sem("q_rank"), sem("q_cnt"), sem("q_zero"), sem("q_zd"),
            sem("q_sl"), sem("q_sc"), sem("q_ord"), sem("q_ot"))

        def wide(a, n):
            return a.unsqueeze(2).to_broadcast([P, T, n])

        with nc.Block() as block:
            @block.vector
            def _(dve):
                chain = Chain(dve, q_ch)

                def tt(out, a, b, op):
                    chain.link(dve.tensor_tensor(out, a, b, op))

                def first(onehot, values, best, weights, n, scratch):
                    chain.link(dve.reduce_max(best, values, axis=X))
                    tt(onehot, values, wide(best, n), ALU.is_equal)
                    tt(scratch, onehot, weights.unsqueeze(1).to_broadcast([P, T, n]), ALU.mult)
                    chain.link(dve.reduce_max(c[:, 11, :], scratch, axis=X))
                    tt(onehot, scratch, wide(c[:, 11, :], n), ALU.is_equal)

                dve.memset(zero[:], 0.0).then_inc(q_zero, 1)
                group = lg[:, :, 0:NGROUPS]
                first(t4[:], group, c[:, 0, :], const(k, "first4"), NGROUPS, u32[:, :, 0:NGROUPS])
                dve.tensor_tensor(t32[:, :, 0:NGROUPS], group, wide(c[:, 0, :], NGROUPS), ALU.subtract).then_inc(q_exp, 1)
                t = le[:].rearrange("p t (g e) -> p t g e", g=NGROUPS)
                src = lg[:, :, NGROUPS:NR].rearrange("p t (g e) -> p t g e", g=NGROUPS)
                tt(t, src, t4[:].unsqueeze(3).to_broadcast([P, T, NGROUPS, PER_GROUP]), ALU.mult)
                chain.link(dve.tensor_scalar(t4[:], t4[:], 1.0, -NEG, ALU.subtract, ALU.mult))
                tt(t, t, t4[:].unsqueeze(3).to_broadcast([P, T, NGROUPS, PER_GROUP]), ALU.add)
                first(one1[:], le[:], c[:, 1, :], const(k, "first32"), EXPERTS, u32[:])
                chain.link(dve.scalar_tensor_tensor(out=le[:], in0=one1[:], scalar=3 * NEG, in1=le[:], op0=ALU.mult, op1=ALU.add))
                first(one2[:], le[:], c[:, 2, :], const(k, "first32"), EXPERTS, u32[:])
                dve.tensor_tensor(c[:, 3, :], c[:, 2, :], c[:, 1, :], ALU.subtract).then_inc(q_exp, 1)
                tt(both[:], one1[:], one2[:], ALU.add)
                tt(both[:], both[:], wide(const(k, "valid"), EXPERTS), ALU.mult)
                chain.link(dve.memset(prefix[:, 0, :], 0.0))
                for i in range(1, T):
                    tt(prefix[:, i, :], prefix[:, i - 1, :], both[:, i - 1, :], ALU.add)
                dve.tensor_tensor(e32[:, 0, :], prefix[:, T - 1, :], both[:, T - 1, :], ALU.add).then_inc(q_both, 1)
                dve.wait_ge(q_cnt, 1)
                chain.link(dve.tensor_scalar(e32[:, 1, :], k.ps[:, 1, 0:EXPERTS], float(BLOCK), 1.0, ALU.max, ALU.subtract))
                chain.link(dve.tensor_copy(ei[:], e32[:, 1, :]))
                chain.link(dve.tensor_single_scalar(ei[:], ei[:], 7, ALU.arith_shift_right))
                chain.link(dve.tensor_copy(e32[:, 2, :], ei[:]))
                chain.link(dve.tensor_copy(e32[:, 3, :], e32[:, 2, :]))
                a, b = 3, 4
                for d in (1, 2, 4, 8, 16):
                    chain.link(dve.tensor_copy(e32[:, b, 0:d], e32[:, a, 0:d]))
                    tt(e32[:, b, d:], e32[:, a, d:], e32[:, a, 0:EXPERTS - d], ALU.add)
                    a, b = b, a
                tt(e32[:, 5, :], e32[:, a, :], e32[:, 2, :], ALU.subtract)
                chain.link(dve.tensor_copy(k.spare_n[:], e32[0:1, a, EXPERTS - 1:EXPERTS]))
                ends = e32[0:1, a, :].unsqueeze(1).to_broadcast([1, SPARE, EXPERTS])
                chain.link(dve.tensor_tensor(spare_f[:], ends, const(k, "iota16", 1).unsqueeze(2).to_broadcast([1, SPARE, EXPERTS]), ALU.is_le))
                chain.link(dve.reduce_sum(e32[0:1, 1, 0:SPARE], spare_f[:], axis=X))
                chain.link(dve.tensor_scalar(e32[0:1, 1, 0:SPARE], e32[0:1, 1, 0:SPARE], float(EXPERTS - 1), None, ALU.min))
                chain.link(dve.tensor_copy(k.spare_of[:], e32[0:1, 1, 0:SPARE]))
                dve.wait_ge(q_rank, 1)
                ranks = k.ps[:, 0, 0:T * EXPERTS].rearrange("p (t e) -> p t e", t=T)
                for j, one in enumerate((one1, one2)):
                    tt(u32[:], one[:], ranks, ALU.mult)
                    chain.link(dve.reduce_sum(c[:, 5, :], u32[:], axis=X))
                    chain.link(dve.tensor_copy(ci[:], c[:, 5, :]))
                    chain.link(dve.tensor_single_scalar(ci[:], ci[:], 7, ALU.arith_shift_right))
                    chain.link(dve.tensor_copy(c[:, 6, :], ci[:]))
                    chain.link(dve.tensor_scalar(c[:, 7, :], c[:, 6, :], 0.0, None, ALU.is_gt))
                    tt(u32[:], one[:], const(k, "iota32").unsqueeze(1).to_broadcast([P, T, EXPERTS]), ALU.mult)
                    chain.link(dve.reduce_sum(c[:, 8, :], u32[:], axis=X))
                    tt(u32[:], one[:], e32[:, 5, :].unsqueeze(1).to_broadcast([P, T, EXPERTS]), ALU.mult)
                    chain.link(dve.reduce_sum(c[:, 9, :], u32[:], axis=X))
                    chain.link(dve.tensor_scalar(c[:, 9, :], c[:, 9, :], float(EXPERTS - 1), None, ALU.add))
                    tt(c[:, 9, :], c[:, 9, :], c[:, 6, :], ALU.add)
                    tt(c[:, 9, :], c[:, 9, :], c[:, 8, :], ALU.subtract)
                    tt(c[:, 9, :], c[:, 9, :], c[:, 7, :], ALU.mult)
                    tt(c[:, 9, :], c[:, 9, :], c[:, 8, :], ALU.add)
                    tt(c[:, 9, :], c[:, 9, :], c[:, 6, :], ALU.subtract)
                    chain.link(dve.scalar_tensor_tensor(out=c[:, 10, :], in0=c[:, 9, :], scalar=float(BLOCK), in1=c[:, 5, :], op0=ALU.mult, op1=ALU.add))
                    dve.tensor_copy(k.slots[:, j, :], c[:, 10, :]).then_inc(q_sl, 1)
                dve.wait_ge(q_ex, 2)
                chain.link(dve.reduce_sum(c[:, 4, :], t32[:, :, 0:NGROUPS], axis=X))
                chain.link(dve.tensor_scalar(c[:, 5, :], c[:, 3, :], 1.0, None, ALU.add))
                tt(c[:, 4, :], c[:, 4, :], c[:, 5, :], ALU.mult)
                chain.link(dve.reciprocal(k.gates[:, 0, :], c[:, 4, :]))
                tt(k.gates[:, 1, :], k.gates[:, 0, :], c[:, 3, :], ALU.mult)
                dve.wait_ge(q_ot, 1)
                dve.tensor_copy(k.order[:], k.ps[:, 2, 0:EXPERTS + SPARE])

            @block.scalar
            def _(act):
                act.wait_ge(q_exp, 1)
                t = t32[:, :, 0:NGROUPS]
                act.activation(t, t, ACT.Exp).then_inc(q_ex, 1)
                act.wait_ge(q_exp, 2)
                act.activation(c[:, 3, :], c[:, 3, :], ACT.Exp).then_inc(q_ex, 1)

            @block.tensor
            def _(pe):
                pe.wait_ge(q_both, 1)
                pe.matmul(k.ps[:, 1, 0:EXPERTS], const(k, "ones"), e32[:, 0, :], start=True, stop=True).then_inc(q_cnt, 1)
                n = T * EXPERTS
                pe.matmul(k.ps[:, 0, 0:n], const(k, "before"), both[:].rearrange("p t e -> p (t e)"), start=True, stop=False)
                pe.matmul(k.ps[:, 0, 0:n], const(k, "ones"), prefix[:].rearrange("p t e -> p (t e)"), start=False, stop=True).then_inc(q_rank, 1)
                pe.wait_ge(q_ord, 16)
                n = EXPERTS + SPARE
                pe.transpose(k.ps[:, 2, 0:n], order_f[:], const(k, "ident")[0:n, 0:n]).then_inc(q_ot, 1)

            @block.gpsimd
            def _(pool):
                pool.wait_ge(q_zd, 16)
                flat = k.order_d.rearrange("b s -> (b s)").unsqueeze(1)
                for j in range(2):
                    pool.wait_ge(q_sl, j + 1)
                    for i in range(T):
                        n = rows_of(i)
                        pool.indirect_dma_start(out=flat, out_offset=bass.IndirectOffsetOnAxis(ap=k.slots[0:n, j, i:i + 1], axis=0),
                                                in_=const(k, "token")[0:n, i:i + 1], in_offset=None).then_inc(q_sc, 16)

            @block.sync
            def _(sp):
                sp.wait_ge(q_zero, 1)
                sp.dma_start(k.order_d, zero[:]).then_inc(q_zd, 16)
                sp.wait_ge(q_sc, 16 * 2 * T)
                sp.dma_start(order_f[:], k.order_d).then_inc(q_ord, 16)
                sp.wait_ge(q_ord, 16)




def experts(nc, k, io):
    HB = DE // P
    E = EXPERTS
    with ExitStack() as ctx:
        def sb(name, shape, dt=F32):
            return ctx.enter_context(nc.sbuf_tensor(name, shape, dt))

        sem = k.sem
        w13 = k.first_w13
        h13, l13 = sb("e_h13", [P, 2, KD, DE], F32R), sb("e_l13", [P, 2, KD, DE], F32R)
        w2 = k.first_w2
        h2, l2 = sb("e_h2", [P, HB, D], F32R), sb("e_l2", [P, HB, D], F32R)
        row = sb("e_row", [P, 1], U32)
        x = sb("e_x", [P, D])
        xh, xl = sb("e_xh", [P, KD, P], F32R), sb("e_xl", [P, KD, P], F32R)
        hid = sb("e_hid", [P, DE])
        hh, hl = sb("e_hh", [P, HB, P], F32R), sb("e_hl", [P, HB, P], F32R)
        y = sb("e_y", [P, D])
        s_w13, s_w2 = [sem("e_w13_0"), sem("e_w13_1")], sem("e_w2_")
        s_row, s_go, s_gp, s_x = sem("e_row_"), sem("e_go"), sem("e_gp"), sem("e_x_")
        s_hi, s_hi2, s_lo, s_lo2, s_use, s_use2 = (sem("e_hi"), sem("e_hi2"), sem("e_lo"), sem("e_lo2"), sem("e_use"),
                                                   sem("e_use2"))
        s_xt, s_xh, s_xl, s_g, s_h, s_ht, s_hh, s_hl, s_yk, s_ys = (
            sem("e_xt"), sem("e_xh_"), sem("e_xl_"), sem("e_g_"), sem("e_h"), sem("e_ht"), sem("e_hh_"),
            sem("e_hl_"), sem("e_yk"), sem("e_ys"))
        W1 = io["w_up"][0].rearrange("e (p k) f -> e p k f", k=KD)
        W3 = io["w_gate"][0].rearrange("e (p k) f -> e p k f", k=KD)
        W2 = io["w_down"][0].rearrange("e (p j) n -> e p j n", j=HB)
        ys = k.ys.rearrange("(b p) n -> b p n", p=BLOCK)

        def one(a, e):
            return a[bass.ds(e, 1)].rearrange("e p ... -> (e p) ...") if not isinstance(e, int) else a[e]

        ident = const(k, "ident")

        def products(pe, out, high, low, w_high, w_low, first, last):
            pe.matmul(out, high, w_high, start=first, stop=False)
            pe.matmul(out, high, w_low, start=False, stop=False)
            return pe.matmul(out, low, w_high, start=False, stop=last)

        def turn_rows(pe):
            xk = x[:].rearrange("p (d k) -> p k d", k=KD)
            for half in range(2):
                for j in range(4):
                    mm = pe.transpose(k.ps[:, half, j * P:(j + 1) * P], xk[:, 4 * half + j, :], ident)
            return mm

        def up(pe, kk):
            for m in range(2):
                mm = products(pe, k.ps[:, 2 + m, :], xh[:, kk, :], xl[:, kk, :], h13[:, m, kk, :], l13[:, m, kk, :],
                              kk == 0, kk == KD - 1)
            return mm

        def turn_hidden(pe):
            hk = hid[:].rearrange("p (d j) -> p j d", j=HB)
            for j in range(HB):
                mm = pe.transpose(k.ps[:, 4, j * P:(j + 1) * P], hk[:, j, :], ident)
            return mm

        def down(pe, j):
            for half in range(2):
                part = slice(512 * half, 512 * (half + 1))
                mm = products(pe, k.ps[:, 5 + half, :], hh[:, j, :], hl[:, j, :], h2[:, j, part], l2[:, j, part],
                              j == 0, j == HB - 1)
            return mm

        turned_rows = k.ps[:, 0:2, :].rearrange("p b n -> p (b n)")
        turned_hidden = k.ps[:, 4, :]

        def flat3(t):
            return t[:].rearrange("p k t -> p (k t)")

        def high13(act, kk):
            return act.copy(h13[:, :, kk, :], w13[:, :, kk, :])

        def low13(dve, kk):
            return dve.tensor_tensor(l13[:, :, kk, :], w13[:, :, kk, :], h13[:, :, kk, :].bitcast(F32), ALU.subtract)

        def high2(act, j):
            return act.copy(h2[:, j, :], w2[:, j, :])

        def low2(dve, j):
            return dve.tensor_tensor(l2[:, j, :], w2[:, j, :], h2[:, j, :].bitcast(F32), ALU.subtract)

        def low_rows(dve):
            return dve.tensor_tensor(flat3(xl), turned_rows, flat3(xh).bitcast(F32), ALU.subtract)

        def low_hidden(dve):
            return dve.tensor_tensor(flat3(hl), turned_hidden, flat3(hh).bitcast(F32), ALU.subtract)

        def silu_gate(act):
            return act.activation(hid[:], k.ps[:, 2, :], ACT.Silu)

        def times_up(dve):
            return dve.tensor_tensor(hid[:], hid[:], k.ps[:, 3, :], ALU.mult)

        def keep_y(act):
            return act.copy(y[:], k.ps[:, 5:7, :].rearrange("p b n -> p (b n)"))

        def rounds_of(eng, round_):
            round_(0, None)
            with eng.Fori(1, E - 1) as e:
                round_(e, e - 1)
            round_(E - 1, E - 2)

        def is_last(e):
            return isinstance(e, int) and e == E - 1

        with nc.Block() as block:
            @block.sync
            def _(sp):
                def load13(e):
                    for half in range(2):
                        part = slice(KD // 2 * half, KD // 2 * (half + 1))
                        sp.wait_ge(s_lo, e * KD - (KD // 2 if half == 0 else 0))
                        sp.sem_inc(s_go, 1)
                        sp.dma_start(w13[:, 0, part], one(W1, e)[:, part]).then_inc(s_w13[half], 16)
                        sp.dma_start(w13[:, 1, part], one(W3, e)[:, part]).then_inc(s_w13[half], 16)

                def load2(e):
                    sp.wait_ge(s_lo2, e * HB)
                    sp.sem_inc(s_go, 1)
                    sp.dma_start(w2[:], one(W2, e)).then_inc(s_w2, 16)

                def store(p):
                    sp.wait_ge(s_yk, p + 2)
                    sp.sem_inc(s_go, 1)
                    sp.dma_start(one(ys, p), y[:]).then_inc(s_ys, 16)

                load13(1)
                load13(2)
                with sp.Fori(1, E - 2) as e:
                    load2(e)
                    load13(e + 2)
                    store(e - 1)
                for e in (E - 2, E - 1):
                    load2(e)
                    store(e - 1)
                store(E - 1)
                sp.wait_ge(s_ys, 16 * (E + 1))

            @block.gpsimd
            def _(pool):
                for half in range(2):
                    pool.sem_inc(s_w13[half], 32)
                pool.sem_inc(s_w2, 16)
                pool.sem_inc(s_yk, 1)
                pool.sem_inc(s_use2, HB)
                pool.sem_inc(s_ys, 16)
                pool.sem_inc(s_xt, 1)
                with pool.Fori(0, E) as e:
                    pool.wait_ge(s_xt, e + 1)
                    pool.tensor_copy(row[:], k.order[:, bass.ds(e, 1)]).then_inc(s_row, 1)
                    pool.wait_ge(s_row, e + 1)
                    pool.sem_inc(s_gp, 1)
                    pool.indirect_dma_start(out=x[:], out_offset=None, in_=k.xn,
                                            in_offset=bass.IndirectOffsetOnAxis(ap=row[:], axis=0)).then_inc(s_x, 16)

            @block.tensor
            def _(pe):
                def step_turn(e):
                    pe.wait_ge(s_x, e * 16 + 16)
                    turn_rows(pe).then_inc(s_xt, 1)

                def step_down(e, p):
                    pe.wait_ge(s_hl, e)
                    pe.wait_ge(s_yk, e)
                    for j in range(HB):
                        pe.wait_ge(s_lo2, p * HB + (j + 1))
                        down(pe, j).then_inc(s_use2, 1)

                def round_(e, p):
                    pe.wait_ge(s_xl, e + 1)
                    for kk in range(KD):
                        pe.wait_ge(s_lo, e * KD + (kk + 1))
                        up(pe, kk).then_inc(s_use, 1)
                    if not is_last(e):
                        step_turn(e + 1)
                    if p is not None:
                        step_down(e, p)
                    pe.wait_ge(s_h, e + 1)
                    turn_hidden(pe).then_inc(s_ht, 1)

                step_turn(0)
                rounds_of(pe, round_)
                step_down(E, E - 1)

            @block.scalar
            def _(act):
                def split13(e, half):
                    for kk in range(KD // 2 * half, KD // 2 * (half + 1)):
                        if kk % (KD // 2) == 0:
                            act.wait_ge(s_w13[half], e * 32 + 64)
                        act.wait_ge(s_use, e * KD + (kk + 1))
                        high13(act, kk).then_inc(s_hi, 1)

                def split2(e):
                    act.wait_ge(s_w2, e * 16)
                    act.wait_ge(s_use2, e * HB)
                    for j in range(HB):
                        high2(act, j).then_inc(s_hi2, 1)

                def output(e):
                    act.wait_ge(s_use2, e * HB + HB)
                    act.wait_ge(s_ys, e * 16)
                    keep_y(act).then_inc(s_yk, 1)

                def round_(e, p):
                    if p is not None:
                        split2(e)
                    if not is_last(e):
                        split13(e, 0)
                        split13(e, 1)
                    act.wait_ge(s_use, e * KD + KD)
                    silu_gate(act).then_inc(s_g, 1)
                    if not is_last(e):
                        act.wait_ge(s_xt, e + 3)
                        act.copy(flat3(xh), turned_rows).then_inc(s_xh, 1)
                    if p is not None:
                        output(e)
                    act.wait_ge(s_ht, e + 1)
                    act.copy(flat3(hh), turned_hidden).then_inc(s_hh, 1)

                for half in range(2):
                    act.wait_ge(s_w13[half], 32)
                for kk in range(KD):
                    high13(act, kk).then_inc(s_hi, 1)
                act.wait_ge(s_xt, 2)
                act.copy(flat3(xh), turned_rows).then_inc(s_xh, 1)
                rounds_of(act, round_)
                split2(E)
                output(E)

            @block.vector
            def _(dve):
                def split13(e, half):
                    for kk in range(KD // 2 * half, KD // 2 * (half + 1)):
                        dve.wait_ge(s_hi, e * KD + (KD + kk + 1))
                        low13(dve, kk).then_inc(s_lo, 1)

                def split2(p):
                    for j in range(HB):
                        dve.wait_ge(s_hi2, p * HB + (j + 1))
                        low2(dve, j).then_inc(s_lo2, 1)

                def round_(e, p):
                    if p is not None:
                        split2(p)
                    if not is_last(e):
                        split13(e, 0)
                        split13(e, 1)
                    dve.wait_ge(s_g, e + 1)
                    times_up(dve).then_inc(s_h, 1)
                    if not is_last(e):
                        dve.wait_ge(s_xh, e + 2)
                        low_rows(dve).then_inc(s_xl, 1)
                    dve.wait_ge(s_hh, e + 1)
                    low_hidden(dve).then_inc(s_hl, 1)

                for kk in range(KD):
                    dve.wait_ge(s_hi, kk + 1)
                    low13(dve, kk).then_inc(s_lo, 1)
                dve.wait_ge(s_xh, 1)
                low_rows(dve).then_inc(s_xl, 1)
                rounds_of(dve, round_)
                split2(E - 1)

        z = {n: sem(f"z_{n}") for n in ("w", "sp", "row", "go", "x", "xt", "xh", "xl", "hi", "hi2", "lo", "lo2", "up", "g", "h",
                                        "ht", "hh", "hl", "dn", "yk", "ys")}

        def spare(eng):
            return eng.value_load(k.spare_n[0:1, 0:1], min_val=0, max_val=SPARE)

        with nc.Block() as block:
            @block.sync
            def _(sp):
                count = spare(sp)
                with sp.If(count > 0):
                    with sp.Fori(0, count) as n:
                        e = sp.value_load(k.spare_of[0:1, bass.ds(n, 1)], min_val=0, max_val=E - 1)
                        sp.wait_ge(z["dn"], n + 1)
                        sp.sem_inc(z["sp"], 1)
                        sp.dma_start(w13[:, 0], one(W1, e)).then_inc(z["w"], 16)
                        sp.dma_start(w13[:, 1], one(W3, e)).then_inc(z["w"], 16)
                        sp.dma_start(w2[:], one(W2, e)).then_inc(z["w"], 16)
                        sp.wait_ge(z["yk"], n + 1)
                        sp.sem_inc(z["sp"], 1)
                        sp.dma_start(one(ys, n + E), y[:]).then_inc(z["ys"], 16)
                        sp.wait_ge(z["ys"], (n + 2) * 16)
                        sp.sem_inc(z["sp"], 1)

            @block.gpsimd
            def _(pool):
                pool.sem_inc(z["dn"], 1)
                pool.sem_inc(z["xt"], 1)
                pool.sem_inc(z["ys"], 16)
                count = spare(pool)
                with pool.If(count > 0):
                    with pool.Fori(0, count) as n:
                        pool.wait_ge(z["xt"], n + 1)
                        pool.tensor_copy(row[:], k.order[:, bass.ds(n + E, 1)]).then_inc(z["row"], 1)
                        pool.wait_ge(z["row"], n + 1)
                        pool.sem_inc(z["go"], 1)
                        pool.indirect_dma_start(out=x[:], out_offset=None, in_=k.xn,
                                                in_offset=bass.IndirectOffsetOnAxis(ap=row[:], axis=0)).then_inc(z["x"], 16)

            @block.tensor
            def _(pe):
                count = spare(pe)
                with pe.If(count > 0):
                    with pe.Fori(0, count) as n:
                        pe.wait_ge(z["x"], (n + 1) * 16)
                        turn_rows(pe).then_inc(z["xt"], 1)
                        pe.wait_ge(z["xl"], n + 1)
                        pe.wait_ge(z["lo"], n + 1)
                        for kk in range(KD):
                            mm = up(pe, kk)
                        mm.then_inc(z["up"], 1)
                        pe.wait_ge(z["h"], n + 1)
                        turn_hidden(pe).then_inc(z["ht"], 1)
                        pe.wait_ge(z["hl"], n + 1)
                        pe.wait_ge(z["lo2"], n + 1)
                        for j in range(HB):
                            mm = down(pe, j)
                        mm.then_inc(z["dn"], 1)

            @block.scalar
            def _(act):
                count = spare(act)
                with act.If(count > 0):
                    with act.Fori(0, count) as n:
                        act.wait_ge(z["w"], (n + 1) * 48)
                        for kk in range(KD):
                            ins = high13(act, kk)
                        ins.then_inc(z["hi"], 1)
                        for j in range(HB):
                            ins = high2(act, j)
                        ins.then_inc(z["hi2"], 1)
                        act.wait_ge(z["xt"], n + 2)
                        act.copy(flat3(xh), turned_rows).then_inc(z["xh"], 1)
                        act.wait_ge(z["up"], n + 1)
                        silu_gate(act).then_inc(z["g"], 1)
                        act.wait_ge(z["ht"], n + 1)
                        act.copy(flat3(hh), turned_hidden).then_inc(z["hh"], 1)
                        act.wait_ge(z["dn"], n + 2)
                        act.wait_ge(z["ys"], (n + 1) * 16)
                        keep_y(act).then_inc(z["yk"], 1)

            @block.vector
            def _(dve):
                count = spare(dve)
                with dve.If(count > 0):
                    with dve.Fori(0, count) as n:
                        dve.wait_ge(z["hi"], n + 1)
                        for kk in range(KD):
                            ins = low13(dve, kk)
                        ins.then_inc(z["lo"], 1)
                        dve.wait_ge(z["hi2"], n + 1)
                        for j in range(HB):
                            ins = low2(dve, j)
                        ins.then_inc(z["lo2"], 1)
                        dve.wait_ge(z["xh"], n + 1)
                        low_rows(dve).then_inc(z["xl"], 1)
                        dve.wait_ge(z["g"], n + 1)
                        times_up(dve).then_inc(z["h"], 1)
                        dve.wait_ge(z["hh"], n + 1)
                        low_hidden(dve).then_inc(z["hl"], 1)




def combine(nc, k, io):
    with ExitStack() as ctx:
        y = ctx.enter_context(nc.sbuf_tensor("c_y", [P, 3, 2, D], F32))
        sem = k.sem
        s_y, s_add, s_out = [sem(f"c_y{j}") for j in range(3)], sem("c_add"), sem("c_out")
        s_half = sem("c_half")
        y_rows = io["y_prompt"][0].rearrange("(i p) d -> i p d", p=P)
        with nc.Block() as block:
            @block.gpsimd
            def _(pool):
                for i in range(TILES):
                    n = NS if i == 0 else P
                    if i >= 3:
                        pool.wait_ge(s_add, i - 2)
                    for j in range(2):
                        pool.indirect_dma_start(out=y[0:n, i % 3, j, :], out_offset=None, in_=k.ys,
                                                in_offset=bass.IndirectOffsetOnAxis(ap=k.slots[0:n, j, i:i + 1], axis=0)).then_inc(s_y[i % 3], 16)

            @block.vector
            def _(dve):
                for i in range(TILES):
                    n = NS if i == 0 else P
                    h = k.h[0:n, i, :]
                    dve.wait_ge(s_y[i % 3], 32 * (i // 3 + 1))
                    dve.scalar_tensor_tensor(out=h, in0=y[0:n, i % 3, 0, :], scalar=k.gates[0:n, 0, i:i + 1], in1=h, op0=ALU.mult,
                                             op1=ALU.add).then_inc(s_half, 1)
                    dve.wait_ge(s_half, i + 1)
                    dve.scalar_tensor_tensor(out=h, in0=y[0:n, i % 3, 1, :], scalar=k.gates[0:n, 1, i:i + 1], in1=h, op0=ALU.mult,
                                             op1=ALU.add).then_inc(s_add, 1)

            @block.sync
            def _(sp):
                for i in range(TILES):
                    sp.wait_ge(s_add, i + 1)
                    if i == 0:
                        sp.dma_start(io["y_sample"].rearrange("b t d -> (b t) d"), k.h[0:NS, 0, :]).then_inc(s_out, 16)
                    else:
                        sp.dma_start(y_rows[i - 1], k.h[:, i, :]).then_inc(s_out, 16)
                sp.wait_ge(s_out, 16 * TILES)


def build(nc, io):
    with ExitStack() as whole, ExitStack() as mixing, ExitStack() as prompt:
        k = Space()
        taken = []

        def sem(name):
            taken.append(nc.alloc_semaphore(name))
            return taken[-1]

        def give_back():
            nc.clear_and_free_semaphores(taken)
            taken.clear()
            nc.all_engine_barrier()

        k.sem = sem

        def sb(name, shape, until=prompt, side=None):
            return until.enter_context(nc.sbuf_tensor(name, shape, F32, side=side))

        k.ps = whole.enter_context(nc.psum_tensor("ps", [P, 8, 512], F32))
        k.ident = sb("ident", [P, P], whole)
        k.neg_lam = sb("neg_lam", [P, 1], whole)
        k.slots = whole.enter_context(nc.sbuf_tensor("slots", [P, 2, TILES], U32))
        k.gates = sb("gates", [P, 2, TILES], whole)
        k.order = whole.enter_context(nc.sbuf_tensor("order", [P, EXPERTS + SPARE], U32))
        k.spare_n = whole.enter_context(nc.sbuf_tensor("spare_n", [1, 1], I32))
        k.spare_of = whole.enter_context(nc.sbuf_tensor("spare_of", [1, SPARE], I32))
        k.consts = sb("other_consts", [P, CONSTS.shape[1] - P], mixing)
        k.new_v, k.kTs = sb("new_v", [NS, W], mixing), sb("kTs", [P, HEADS, NS], mixing)
        k.qTs = sb("qTs", [P, HEADS, NS], mixing)
        k.qk = sb("qk", [P, TILES, W])
        k.sample_v = sb("sample_v", [NS, W])
        k.z = sb("z", [P, TILES, GW])
        k.meta_qk, k.meta_v = sb("meta_qk", [META, W]), sb("meta_v", [META, W])
        k.meta_dv, k.meta_z = sb("meta_dv", [META, W]), sb("meta_z", [META, GW])
        k.kT, k.qT = sb("kT", [P, HEADS, SEQ]), sb("qT", [P, HEADS, SEQ])
        k.meta_kT = sb("meta_kT", [P, HEADS, META])
        k.ys = nc.dram_tensor("ys_d", ((EXPERTS + SPARE) * BLOCK, D), F32, kind="Internal").ap()
        k.v_d = nc.dram_tensor("v_d", (TILES, P, W), F32, kind="Internal").ap()
        k.gate_d = nc.dram_tensor("gate_d", (TILES, P, W), F32, kind="Internal").ap()
        project(nc, k, io)
        k.v, k.dv = sb("v", [P, TILES, W]), sb("dv", [P, TILES, W])
        k.cat = sb("cat", [P, TILES, D], whole, "right")
        linear_attention(nc, k, io)
        sample_linear_attention(nc, k, io)
        prompt_attention(nc, k, io)
        prompt.close()
        give_back()
        k.wr, k.br = sb("wr", [P, KD, NR], mixing), sb("br", [P, NR], mixing)
        k.gain2, k.head_gain = sb("gain2", [P, D], mixing), sb("head_gain", [P, 2], mixing)
        sample_attention(nc, k, io)
        k.h = k.cat
        k.xn = nc.dram_tensor("xn_d", (TOKENS, D), F32, kind="Internal").ap()
        k.order_d = nc.dram_tensor("order_d", (EXPERTS + SPARE, BLOCK), F32, kind="Internal").ap()
        k.first_w13 = sb("first_w13", [P, 2, KD, DE], whole, "right")
        k.first_w2 = sb("first_w2", [P, DE // P, D], whole, "right")
        merge_and_route(nc, k, io)
        mixing.close()
        give_back()
        experts(nc, k, io)
        combine(nc, k, io)


_OUTS = [("y_prompt", (1, SEQ, D)), ("y_sample", (SAMPLES, STEPS, D)),
         ("k_prompt", (1, META + SEQ, 1, HEADS, P)), ("v_prompt", (1, META + SEQ, 1, HEADS, P)),
         ("gla_prompt", (1, 1, HEADS, DK, DV)), ("k_sample", (SAMPLES, STEPS, 1, HEADS, P)),
         ("v_sample", (SAMPLES, STEPS, 1, HEADS, P)), ("gla_sample", (SAMPLES, 1, HEADS, DK, DV))]


def kernel(**inputs):
    import concourse.bacc as _bacc
    from concourse.bass_utils import run_bass_kernel_spmd as _run

    nc = _bacc.Bacc("TRN2", target_bir_lowering=False, num_devices=1)
    arrays, io = {}, {}
    for name, a in [*inputs.items(), ("consts", CONSTS)]:
        a = np.ascontiguousarray(a)
        arrays[f"in_{name}"] = a
        io[name] = nc.dram_tensor(f"in_{name}", a.shape, mybir.dt.from_np(a.dtype), kind="ExternalInput").ap()
    for name, shape in _OUTS:
        io[name] = nc.dram_tensor(f"out_{name}", shape, F32, kind="ExternalOutput").ap()
    build(nc, io)
    r = _run(nc, [arrays], core_ids=[0])
    return tuple(r.results[0][f"out_{name}"] for name, _ in _OUTS)
```
